# Optimizing a Trainium2 kernel written in Bass

```python
import jax, jax.numpy as jnp
from jax import lax
import numpy as np

D_MODEL = 1024
BATCH = 1
SEQ = 1024
DEPTH = 1
DEC_BATCH = 1
DEC_SEQ = 32
PAST_LEN = 256

CHUNK = 64
HEAD_DIM = 64
A_HEADS = 8
A_WIDTH = A_HEADS * HEAD_DIM
B_WIDTH = 256
CONV_W = 3
M_HEADS = 4
M_WIDTH = M_HEADS * HEAD_DIM
N_MEM = 256
MIX_WIDTH = A_WIDTH + B_WIDTH + M_WIDTH
IN_COLS = 3 * A_WIDTH + A_HEADS + 3 * B_WIDTH + M_WIDTH
Q_BLOCK = 128
PEER_HEADS = 8
PEER_KEYS = 128
PEER_N = PEER_KEYS * PEER_KEYS
PEER_QDIM = 128
PEER_HALF = PEER_QDIM // 2
PEER_TOPK = 16
PEER_BLOCK = 128
EPS = 1e-6

kernel_name = 'fox_shortconv_memory_peer_stream_step'

def rmsnorm(x, g):
    xf = x.astype(jnp.float32)
    y = xf * lax.rsqrt(jnp.mean(xf * xf, axis=-1, keepdims=True) + EPS)
    return (y * g.astype(jnp.float32)).astype(x.dtype)

def _in_splits():
    sizes = [A_WIDTH, A_WIDTH, A_WIDTH, A_HEADS, B_WIDTH, B_WIDTH, B_WIDTH, M_WIDTH]
    return [int(c) for c in np.cumsum(sizes)[:-1]]

def mixer_inputs(h, w_in, b_f, g_qa, g_ka, g_qm):
    b, t = h.shape[0], h.shape[1]
    z = h @ w_in
    qa, ka, va, fl, bg, cg, hv, qm = jnp.split(z, _in_splits(), axis=-1)
    qa = rmsnorm(qa.reshape(b, t, A_HEADS, HEAD_DIM), g_qa)
    ka = rmsnorm(ka.reshape(b, t, A_HEADS, HEAD_DIM), g_ka)
    va = va.reshape(b, t, A_HEADS, HEAD_DIM)
    logf = jax.nn.log_sigmoid(fl.astype(jnp.float32) + b_f.astype(jnp.float32))
    qm = rmsnorm(qm.reshape(b, t, M_HEADS, HEAD_DIM), g_qm)
    return qa, ka, va, logf, bg, cg * hv, qm

def fox_attend(q, k, v, fq, fk, q_pos, k_pos):
    s = jnp.einsum('bqhd,bkhd->bhqk', q, k).astype(jnp.float32) * (HEAD_DIM ** -0.5)
    s = s + jnp.transpose(fq, (0, 2, 1))[:, :, :, None] - jnp.transpose(fk, (0, 2, 1))[:, :, None, :]
    mask = k_pos[None, :] <= q_pos[:, None]
    s = jnp.where(mask[None, None], s, -jnp.inf)
    p = jax.nn.softmax(s, axis=-1).astype(v.dtype)
    return jnp.einsum('bhqk,bkhd->bqhd', p, v)

def fox_prompt(q, k, v, F):
    b, s = q.shape[0], q.shape[1]
    nb = s // Q_BLOCK
    qb = q.reshape(b, nb, Q_BLOCK, A_HEADS, HEAD_DIM).transpose(1, 0, 2, 3, 4)
    fb = F.reshape(b, nb, Q_BLOCK, A_HEADS).transpose(1, 0, 2, 3)
    k_pos = jnp.arange(s)

    def one(args):
        i, qi, fi = args
        q_pos = i * Q_BLOCK + jnp.arange(Q_BLOCK)
        return fox_attend(qi, k, v, fi, F, q_pos, k_pos)

    out = lax.map(one, (jnp.arange(nb), qb, fb))
    return out.transpose(1, 0, 2, 3, 4).reshape(b, s, A_WIDTH)

def short_conv(u, prev, w, bias):
    t = u.shape[1]
    up = jnp.concatenate([prev.astype(u.dtype), u], axis=1)
    y = bias + w[CONV_W - 1] * up[:, CONV_W - 1:CONV_W - 1 + t]
    for j in range(CONV_W - 1):
        y = y + w[j] * up[:, j:j + t]
    return y, up[:, -(CONV_W - 1):]

def memory_kv(mem, g_mem, w_mk, w_mv, g_km):
    bm = mem.shape[0]
    hm = rmsnorm(mem, g_mem)
    mk = rmsnorm((hm @ w_mk).reshape(bm, N_MEM, M_HEADS, HEAD_DIM), g_km)
    mv = (hm @ w_mv).reshape(bm, N_MEM, M_HEADS, HEAD_DIM)
    return mk, mv

def memory_attend(q, mk, mv):
    b, t = q.shape[0], q.shape[1]
    s = jnp.einsum('bqhd,bkhd->bhqk', q, mk).astype(jnp.float32) * (HEAD_DIM ** -0.5)
    p = jax.nn.softmax(s, axis=-1).astype(mv.dtype)
    return jnp.einsum('bhqk,bkhd->bqhd', p, mv).reshape(b, t, M_WIDTH)

def merge_out(oa, ob, om, w_out):
    return jnp.concatenate([oa, ob, om], axis=-1) @ w_out

def peer_tokens(xt, w_pq, keys, u_tab, v_tab):
    n = xt.shape[0]
    q = (xt @ w_pq).reshape(n, PEER_HEADS, 2, PEER_HALF)
    s = jnp.einsum('nhpd,hpkd->nhpk', q, keys).astype(jnp.float32)
    s1, i1 = lax.top_k(s[:, :, 0], PEER_TOPK)
    s2, i2 = lax.top_k(s[:, :, 1], PEER_TOPK)
    cand = (s1[..., :, None] + s2[..., None, :]).reshape(n, PEER_HEADS, PEER_TOPK * PEER_TOPK)
    sc, ci = lax.top_k(cand, PEER_TOPK)
    e = (jnp.take_along_axis(i1, ci // PEER_TOPK, axis=-1) * PEER_KEYS
         + jnp.take_along_axis(i2, ci % PEER_TOPK, axis=-1))
    g = jax.nn.softmax(sc, axis=-1)
    a = jax.nn.gelu(jnp.einsum('nhkd,nd->nhk', u_tab[e], xt).astype(jnp.float32), approximate=False)
    wgt = (g * a).astype(xt.dtype)
    return jnp.einsum('nhk,nhkd->nd', wgt, v_tab[e])

def peer(x, w_pq, keys, u_tab, v_tab):
    b, t, d = x.shape
    n = b * t
    nb = -(-n // PEER_BLOCK)
    xt = jnp.pad(x.reshape(n, d), ((0, nb * PEER_BLOCK - n), (0, 0)))
    out = lax.map(lambda xb: peer_tokens(xb, w_pq, keys, u_tab, v_tab), xt.reshape(nb, PEER_BLOCK, d))
    return out.reshape(nb * PEER_BLOCK, d)[:n].reshape(b, t, d)

def setup_inputs(seed: int = 0) -> dict:
    key = jax.random.key(seed)
    ks = iter(jax.random.split(key, 32))

    def nrm(shape, scale):
        return jax.random.normal(next(ks), shape, jnp.float32) * scale

    forget_bias = jnp.linspace(1.0, 5.0, A_HEADS, dtype=jnp.float32)
    return {
        'x_prompt': nrm((BATCH, SEQ, D_MODEL), 1.0),
        'x_sample': nrm((DEC_BATCH, DEC_SEQ, D_MODEL), 1.0),
        'cache_a_k': nrm((DEPTH, DEC_BATCH, PAST_LEN, A_HEADS, HEAD_DIM), 1.0),
        'cache_a_v': nrm((DEPTH, DEC_BATCH, PAST_LEN, A_HEADS, HEAD_DIM), 1.0),
        'cache_a_logf': jax.nn.log_sigmoid(nrm((DEPTH, DEC_BATCH, PAST_LEN, A_HEADS), 1.0) + forget_bias),
        'cache_b_conv': nrm((DEPTH, DEC_BATCH, CONV_W - 1, B_WIDTH), 0.5),
        'cache_m_k': nrm((DEPTH, DEC_BATCH, N_MEM, M_HEADS, HEAD_DIM), 1.0),
        'cache_m_v': nrm((DEPTH, DEC_BATCH, N_MEM, M_HEADS, HEAD_DIM), 1.0),
        'mem_prompt': nrm((BATCH, N_MEM, D_MODEL), 1.0),
        'g_attn': 1.0 + nrm((DEPTH, D_MODEL), 0.02),
        'w_in': nrm((DEPTH, D_MODEL, IN_COLS), D_MODEL ** -0.5),
        'b_f': forget_bias[None, :] + nrm((DEPTH, A_HEADS), 0.1),
        'g_q_a': 1.0 + nrm((DEPTH, HEAD_DIM), 0.02),
        'g_k_a': 1.0 + nrm((DEPTH, HEAD_DIM), 0.02),
        'conv_w': nrm((DEPTH, CONV_W, B_WIDTH), CONV_W ** -0.5),
        'conv_b': nrm((DEPTH, B_WIDTH), 0.02),
        'g_mem': 1.0 + nrm((DEPTH, D_MODEL), 0.02),
        'w_mem_k': nrm((DEPTH, D_MODEL, M_WIDTH), D_MODEL ** -0.5),
        'w_mem_v': nrm((DEPTH, D_MODEL, M_WIDTH), D_MODEL ** -0.5),
        'g_k_m': 1.0 + nrm((DEPTH, HEAD_DIM), 0.02),
        'g_q_m': 1.0 + nrm((DEPTH, HEAD_DIM), 0.02),
        'w_out': nrm((DEPTH, MIX_WIDTH, D_MODEL), 0.5 * MIX_WIDTH ** -0.5),
        'g_ffn': 1.0 + nrm((DEPTH, D_MODEL), 0.02),
        'w_peer_q': nrm((DEPTH, D_MODEL, PEER_HEADS * PEER_QDIM), D_MODEL ** -0.5),
        'peer_keys': nrm((DEPTH, PEER_HEADS, 2, PEER_KEYS, PEER_HALF), PEER_HALF ** -0.5),
        'peer_u': nrm((DEPTH, PEER_N, D_MODEL), D_MODEL ** -0.5),
        'peer_v': nrm((DEPTH, PEER_N, D_MODEL), PEER_HEADS ** -0.5),
    }

def reference(x_prompt, x_sample, cache_a_k, cache_a_v, cache_a_logf, cache_b_conv, cache_m_k, cache_m_v,
              mem_prompt, g_attn, w_in, b_f, g_q_a, g_k_a, conv_w, conv_b, g_mem, w_mem_k, w_mem_v,
              g_k_m, g_q_m, w_out, g_ffn, w_peer_q, peer_keys, peer_u, peer_v):
    xp, xs = x_prompt, x_sample
    akp, avp, alp, bcp, mkp, mvp = [], [], [], [], [], []
    aks, avs, als, bcs = [], [], [], []
    for l in range(DEPTH):
        bp = xp.shape[0]
        h = rmsnorm(xp, g_attn[l])
        qa, ka, va, logf, bg, u, qm = mixer_inputs(h, w_in[l], b_f[l], g_q_a[l], g_k_a[l], g_q_m[l])
        F = jnp.cumsum(logf, axis=1)
        oa = fox_prompt(qa, ka, va, F)
        cy, conv_state = short_conv(u, jnp.zeros((bp, CONV_W - 1, B_WIDTH), u.dtype), conv_w[l], conv_b[l])
        mk, mv = memory_kv(mem_prompt, g_mem[l], w_mem_k[l], w_mem_v[l], g_k_m[l])
        om = memory_attend(qm, mk, mv)
        xp = xp + merge_out(oa, bg * cy, om, w_out[l])
        xp = xp + peer(rmsnorm(xp, g_ffn[l]), w_peer_q[l], peer_keys[l], peer_u[l], peer_v[l])
        akp.append(ka); avp.append(va); alp.append(logf); bcp.append(conv_state)
        mkp.append(mk); mvp.append(mv)

        bs, ts = xs.shape[0], xs.shape[1]
        past = cache_a_k.shape[2]
        h = rmsnorm(xs, g_attn[l])
        qa, ka, va, logf, bg, u, qm = mixer_inputs(h, w_in[l], b_f[l], g_q_a[l], g_k_a[l], g_q_m[l])
        k_all = jnp.concatenate([cache_a_k[l].astype(ka.dtype), ka], axis=1)
        v_all = jnp.concatenate([cache_a_v[l].astype(va.dtype), va], axis=1)
        F = jnp.cumsum(jnp.concatenate([cache_a_logf[l].astype(jnp.float32), logf], axis=1), axis=1)
        oa = fox_attend(qa, k_all, v_all, F[:, past:], F,
                        past + jnp.arange(ts), jnp.arange(past + ts)).reshape(bs, ts, A_WIDTH)
        cy, conv_state = short_conv(u, cache_b_conv[l], conv_w[l], conv_b[l])
        om = memory_attend(qm, cache_m_k[l].astype(qm.dtype), cache_m_v[l].astype(qm.dtype))
        xs = xs + merge_out(oa, bg * cy, om, w_out[l])
        xs = xs + peer(rmsnorm(xs, g_ffn[l]), w_peer_q[l], peer_keys[l], peer_u[l], peer_v[l])
        aks.append(ka); avs.append(va); als.append(logf); bcs.append(conv_state)

    return (xp, xs,
            jnp.stack(akp), jnp.stack(avp), jnp.stack(alp), jnp.stack(bcp), jnp.stack(mkp), jnp.stack(mvp),
            jnp.stack(aks), jnp.stack(avs), jnp.stack(als), jnp.stack(bcs))


_drawn_inputs = setup_inputs


def setup_inputs(seed=0):
    import zlib

    import numpy as np

    out = dict(_drawn_inputs(seed))
    spreads = {}
    factors = {'g_q_a': 7.301,
     'g_k_a': 2.813,
     'conv_b': 4.364,
     'g_mem': 2.827,
     'g_k_m': 2.814,
     'g_q_m': 8.0}
    for name, (base, spread) in spreads.items():
        noise = np.random.default_rng([zlib.crc32(name.encode()), seed]).standard_normal(out[name].shape)
        drawn = base * np.exp(spread * noise) if base else spread * noise
        out[name] = __import__('jax').numpy.asarray(drawn.astype(out[name].dtype))
    for name, factor in factors.items():
        out[name] = (out[name] * factor).astype(out[name].dtype)
    return out
```

```python
from contextlib import ExitStack

import concourse.bass as bass
from concourse import mybir

F32 = mybir.dt.float32
U32 = mybir.dt.uint32
ALU = mybir.AluOpType
ACT = mybir.ActivationFunctionType
AX = mybir.AxisListType.X

P = 128
D = 1024
KB = D // P
SEQ, NEW, PAST, NMEM = 1024, 32, 256, 256
TILES = SEQ // P
AH, MH, HD = 8, 4, 64
AW, BW, MW = AH * HD, 256, MH * HD
FCOL = 3 * AW
BCOL = FCOL + AH
CHUNK = 512
PH, PKEYS, TOPK = 8, 128, 16
SLOTS = PH * TOPK
NEXP = PKEYS * PKEYS
EPS = 1e-6
NEG = -1e30
GONE = -3e38
UNITS = AH + MH
NU, NV, ND = 8, 4, 4
VLAG = 24
STEPS = SLOTS + VLAG


class Chain:

    def __init__(self, eng, sem):
        self.eng, self.sem, self.n = eng, sem, 0

    def do(self, ins):
        self.n += 1
        ins.then_inc(self.sem, 1)
        self.eng.wait_ge(self.sem, self.n)


PARTS = (["norm"] * 1 + ["turn", "q", "k", "v", "bc", "hm", "qknorm", "turnqk"] + [f"att{n}" for n in range(UNITS + 1)]
         + ["mix", "out0", "out1", "norm2", "turn2", "pq0", "pq1"] + [f"top{h}" for h in range(PH + 1)])
WEIGHT = {"q": 4, "k": 4, "v": 4, "bc": 4, "hm": 4, "out0": 4, "out1": 4, "pq0": 4, "pq1": 4, "norm": 0, "turn": 1}


def part_steps():
    at, steps, total = 0, {}, sum(WEIGHT.get(p, 3) for p in PARTS)
    for p in PARTS:
        steps[p] = at * (SLOTS - 4) // total
        at += WEIGHT.get(p, 3)
    return steps


AT = part_steps()


def beside(experts, prepare):
    for n in experts:
        while prepare is not None:
            if prepare[1] is None or AT[prepare[1]] <= n:
                prepare[1] = next(prepare[0], False)
                if prepare[1] is False:
                    prepare = None
            else:
                break
    if prepare is not None:
        for _ in prepare[0]:
            pass


class Tile:

    def __init__(self, rows, y_out):
        self.rows, self.y_out = rows, y_out


class NextTile:

    def __init__(self, rows, blocks, sample, x_in, own_keys, own_keysT, own_negF, own_values, k_out, v_out, logf_out, conv_out):
        self.rows, self.blocks, self.sample, self.x_in = rows, blocks, sample, x_in
        self.own_keys, self.own_keysT, self.own_negF, self.own_values = own_keys, own_keysT, own_negF, own_values
        self.k_out, self.v_out, self.logf_out, self.conv_out = k_out, v_out, logf_out, conv_out


def build(nc, d_x_prompt, d_x_sample, d_cache_a_k, d_cache_a_v, d_cache_a_logf, d_cache_b_conv, d_cache_m_k, d_cache_m_v, d_mem_prompt, d_g_attn, d_w_in, d_b_f, d_g_q_a, d_g_k_a, d_conv_w, d_conv_b, d_g_mem, d_w_mem_k, d_w_mem_v, d_g_k_m, d_g_q_m, d_w_out, d_g_ffn, d_w_peer_q, d_peer_keys, d_peer_u, d_peer_v,
          d_y_prompt, d_y_sample, d_a_k, d_a_v, d_a_logf, d_b_conv, d_m_k, d_m_v, d_a_k_s, d_a_v_s, d_a_logf_s, d_b_conv_s):
    with ExitStack() as ctx:
        def sb(name, shape, dt=F32):
            return ctx.enter_context(nc.sbuf_tensor(name, shape, dt))

        ident = sb("ident", [P, P])
        upto = sb("upto", [P, P])
        causal = sb("causal", [P, P])
        headrow = sb("headrow", [P, AH, P])
        iota16 = sb("iota16", [P, TOPK])
        g_attn = sb("g_attn", [P, KB])
        g_mem = sb("g_mem", [P, KB])
        g_ffn = sb("g_ffn", [P, D])
        g_q = sb("g_q", [P, HD])
        g_k = sb("g_k", [P, HD])
        g_qm = sb("g_qm", [P, HD])
        g_km = sb("g_km", [P, HD])
        bias_f = sb("bias_f", [P, AH])
        conv_w = sb("conv_w", [P, 2, 3])
        conv_b = sb("conv_b", [P, 2])
        w_f = sb("w_f", [P, KB, AH])
        keys2 = sb("keys2", [P, PH, 2 * PKEYS])
        kT = sb("kT", [P, AH // 2, SEQ])
        v_all = sb("v_all", [P, TILES, AW])
        negF = sb("negF", [P, SEQ])
        ncarry = sb("ncarry", [AH, 1])
        mkT = sb("mkT", [P, MH // 2, NMEM])
        mv = sb("mv", [P, NMEM // P, MW])
        wbuf = sb("wbuf", [P, 2, KB, CHUNK])
        x = sb("x", [P, D])
        xn = sb("xn", [P, D])
        hT = sb("hT", [P, KB, P])
        mixT = sb("mixT", [P, KB, P])
        z = sb("z", [P, 3 * AW + MW])
        qT = sb("qT", [P, UNITS, P])
        pr = sb("pr", [P, SEQ])
        pT = sb("pT", [P, TILES, P])
        uT = sb("uT", [P, 2, 2 + P])
        bcT = sb("bcT", [P, 4, P])
        yT = sb("yT", [P, 2, P])
        ss = sb("ss", [P, 1])
        rstd = sb("rstd", [P, 1])
        hss = sb("hss", [P, 20])
        hrs = sb("hrs", [P, 20])
        lf = sb("lf", [P, 4, AH])
        logf = sb("logf", [P, 2, AH])
        nmax = sb("nmax", [P, UNITS])
        rsum = sb("rsum", [P, UNITS])
        rinv = sb("rinv", [P, UNITS])
        pick = sb("pick", [P, 2, TOPK])
        picki = sb("picki", [P, 2, TOPK], U32)
        pickf = sb("pickf", [P, 2, TOPK])
        left = sb("left", [P, 2, PKEYS])
        onehot = pr[:, 0:512].rearrange("p (q i j) -> p q i j", q=2, i=TOPK)
        cand = pr[:, 512:768].rearrange("p (i j) -> p i j", i=TOPK)
        candleft = pr[:, 768:1024]
        ci = sb("ci", [P, TOPK], U32)
        cij = sb("cij", [P, 2, TOPK], U32)
        cijf = sb("cijf", [P, 2, TOPK])
        e12 = sb("e12", [P, 2, TOPK])
        sc = sb("sc", [P, PH, TOPK])
        ex = sb("ex", [P, PH, TOPK])
        esum = sb("esum", [P, PH])
        x2n = sb("x2n", [P, D])
        xtn = sb("xtn", [P, D])
        idxn = sb("idxn", [P, PH, TOPK], U32)
        gaten = sb("gaten", [P, PH, TOPK])
        x2 = sb("x2", [P, D])
        xt = sb("xt", [P, D])
        idx = sb("idx", [P, SLOTS], U32)
        gate = sb("gate", [P, PH, TOPK])
        urow = sb("urow", [P, NU, D])
        vrow = sb("vrow", [P, NV, D])
        act = sb("act", [P, PH, TOPK])
        gel = sb("gel", [P, PH, TOPK])
        wgt = sb("wgt", [P, SLOTS])
        diag = sb("diag", [P, ND, P])

        def ps(name, shape):
            return ctx.enter_context(nc.psum_tensor(name, shape, F32))

        acc = ps("acc", [P, D])
        S = ps("S", [P, SEQ])
        tp = ps("tp", [P, KB, P])
        g = [ps("g0", [P, CHUNK]), ps("g1", [P, CHUNK])]

        def sem(name):
            return ctx.enter_context(nc.semaphore(name))

        const_loaded = sem("const_loaded")
        const_made = sem("const_made")
        zeroed = sem("zeroed")
        gains = sem("gains")
        x_loaded = sem("x_loaded")
        xn_ready = sem("xn_ready")
        sq_done = sem("sq_done")
        rms_ready = sem("rms_ready")
        turned = sem("turned")
        hT_ready = sem("hT_ready")
        fl_done = sem("fl_done")
        gemm_done = sem("gemm_done")
        z_ready = sem("z_ready")
        bcT_ready = sem("bcT_ready")
        qk_squares = sem("qk_squares")
        qk_rms = sem("qk_rms")
        qkn_ready = sem("qkn_ready")
        qk_turned = sem("qk_turned")
        qT_ready = sem("qT_ready")
        kT_ready = sem("kT_ready")
        qm_turned = sem("qm_turned")
        qmT_ready = sem("qmT_ready")
        f_ready = sem("f_ready")
        f_exp = sem("f_exp")
        f_ln = sem("f_ln")
        logf_ready = sem("logf_ready")
        cum_done = sem("cum_done")
        cum_used = sem("cum_used")
        s_done = sem("s_done")
        nmax_ready = sem("nmax_ready")
        exp_done = sem("exp_done")
        p_turned = sem("p_turned")
        pT_low = sem("pT_low")
        pT_high = sem("pT_high")
        pv_done = sem("pv_done")
        mix_ready = sem("mix_ready")
        mix_turned = sem("mix_turned")
        mixT_ready = sem("mixT_ready")
        u_ready = sem("u_ready")
        conv_ready = sem("conv_ready")
        x2_ready = sem("x2_ready")
        sq2_done = sem("sq2_done")
        rms2_ready = sem("rms2_ready")
        xt_ready = sem("xt_ready")
        xt_turned = sem("xt_turned")
        xtT_ready = sem("xtT_ready")
        pqT_ready = sem("pqT_ready")
        key_scores = sem("key_scores")
        picked = sem("picked")
        diff_ready = sem("diff_ready")
        ex_ready = sem("ex_ready")
        stored = sem("stored")
        copied = sem("copied")
        dots = sem("dots")
        gelu_done = sem("gelu_done")
        wgt_ready = sem("wgt_ready")
        diag_ready = sem("diag_ready")
        v_used = sem("v_used")
        acc_done = sem("acc_done")
        y_ready = sem("y_ready")
        y_stored = sem("y_stored")
        dve_chain = sem("dve_chain")
        pool_chain = sem("pool_chain")
        cache_loaded = sem("cache_loaded")
        cache_turned = sem("cache_turned")
        cache_copied = sem("cache_copied")
        ft_done = sem("ft_done")
        ft_used = sem("ft_used")
        mm_loaded = sem("mm_loaded")
        w_loaded = [sem(f"w_loaded{i}") for i in range(2)]
        u_landed = [sem(f"u_landed{i}") for i in range(NU)]
        v_landed = [sem(f"v_landed{i}") for i in range(NV)]
        first, last = const_loaded.num, v_landed[NV - 1].num
        every_semaphore = range(first, last + 1)
        assert len(every_semaphore) == 69 + 2 + NU + NV

        def end_block():
            nc.all_engine_barrier(sems_to_clear=every_semaphore)

        def load_chunk(sp, c, srcs, used):
            if c >= 2:
                sp.wait_ge(used, c - 1)
            at = 0
            for src in srcs:
                w = src.shape[1]
                sp.dma_start(wbuf[:, c % 2, :, at:at + w],
                             src.rearrange("(k p) n -> p k n", p=P)).then_inc(w_loaded[c % 2], 16 // len(srcs))
                at += w

        def setup():
            with nc.Block() as block:
                @block.sync
                def _(sp):
                    loads = [(g_attn[:, :], d_g_attn[0].rearrange("(k p) -> p k", p=P)),
                             (g_mem[:, :], d_g_mem[0].rearrange("(k p) -> p k", p=P)),
                             (g_ffn[:, :], d_g_ffn[0].partition_broadcast(P)),
                             (g_q[:, :], d_g_q_a[0].partition_broadcast(P)),
                             (g_k[:, :], d_g_k_a[0].partition_broadcast(P)),
                             (g_qm[:, :], d_g_q_m[0].partition_broadcast(P)),
                             (g_km[:, :], d_g_k_m[0].partition_broadcast(P)),
                             (bias_f[:, :], d_b_f[0].partition_broadcast(P)),
                             (w_f[:, :, :], d_w_in[0][:, FCOL:BCOL].rearrange("(k p) n -> p k n", p=P))]
                    for j in range(3):
                        loads.append((conv_w[:, :, j], d_conv_w[0][j].rearrange("(b p) -> p b", p=P)))
                    loads.append((conv_b[:, :], d_conv_b[0].rearrange("(b p) -> p b", p=P)))
                    with nc.allow_non_contiguous_dma("vectors laid along partitions, once"):
                        for dst, src in loads:
                            sp.dma_start(dst, src).then_inc(const_loaded, 16)
                    sp.dma_start(wbuf[:, 0, :, 0:MW], d_w_mem_k[0].rearrange("(k p) n -> p k n", p=P)).then_inc(mm_loaded, 16)
                    sp.dma_start(wbuf[:, 0, :, MW:2 * MW], d_w_mem_v[0].rearrange("(k p) n -> p k n", p=P)).then_inc(mm_loaded, 16)
                    sp.dma_start(z[:, 0:D].rearrange("p (g d) -> p g d", d=HD),
                                 d_peer_keys[0].rearrange("h q k d -> k (h q) d")).then_inc(cache_loaded, 16)
                    for i in range(2):
                        if i:
                            sp.wait_ge(xn_ready, 1)
                        sp.dma_start(x[:, :], d_mem_prompt[0][i * P:(i + 1) * P, :]).then_inc(x_loaded, 16)
                        sp.wait_ge(qkn_ready, i + 1)
                        sp.dma_start(d_m_k[0][0][i * P:(i + 1) * P].rearrange("n h d -> n (h d)"), xn[:, 0:MW]).then_inc(stored, 16)
                        sp.dma_start(d_m_v[0][0][i * P:(i + 1) * P].rearrange("n h d -> n (h d)"), mv[:, i, :]).then_inc(stored, 16)
                    sp.wait_ge(stored, 64)
                    sp.wait_ge(const_loaded, 16 * len(loads))

                @block.gpsimd
                def _(pool):
                    chain = Chain(pool, pool_chain)
                    chain.do(pool.memset(ident[:, :], 0.0))
                    chain.do(pool.affine_select(ident[:, :], ident[:, :], [[-1, P]], ALU.not_equal, 1.0, base=0, channel_multiplier=1))
                    chain.do(pool.memset(upto[:, :], 1.0))
                    chain.do(pool.affine_select(upto[:, :], upto[:, :], [[1, P]], ALU.is_ge, 0.0, base=0, channel_multiplier=-1))
                    chain.do(pool.memset(causal[:, :], 0.0))
                    chain.do(pool.affine_select(causal[:, :], causal[:, :], [[-1, P]], ALU.is_ge, NEG, base=0, channel_multiplier=1))
                    chain.do(pool.memset(headrow[:, :, :], 0.0))
                    chain.do(pool.affine_select(headrow[:, :, :], headrow[:, :, :], [[-1, AH], [0, P]], ALU.not_equal, 1.0, base=0, channel_multiplier=1))
                    pool.iota(iota16[:, :], [[1, TOPK]], base=0, channel_multiplier=0,
                              allow_small_or_imprecise_dtypes=True).then_inc(const_made, 1)

                @block.vector
                def _(v):
                    chain = Chain(v, dve_chain)
                    v.memset(kT[:, :, :], 0.0).then_inc(zeroed, 1)
                    v.memset(v_all[:, :, :], 0.0).then_inc(zeroed, 1)
                    chain.do(v.memset(negF[:, :], 0.0))
                    v.memset(negF[0:AH, :], NEG).then_inc(zeroed, 1)
                    v.memset(ncarry[:, :], 0.0).then_inc(zeroed, 1)
                    v.memset(qT[:, :, :], 0.0).then_inc(zeroed, 1)
                    v.memset(uT[:, :, :], 0.0).then_inc(zeroed, 1)
                    chain.do(v.memset(keys2[:, :, :], 0.0))
                    v.wait_ge(const_loaded, 16 * 13)
                    v.tensor_scalar(g_q[:, :], g_q[:, :], HD ** -0.5, None, ALU.mult).then_inc(gains, 1)
                    v.tensor_scalar(g_qm[:, :], g_qm[:, :], HD ** -0.5, None, ALU.mult).then_inc(gains, 1)
                    v.wait_ge(cache_turned, 1)
                    v.tensor_copy(keys2[0:HD, :, 0:PKEYS], tp[0:HD, :, :]).then_inc(cache_copied, 1)
                    v.tensor_copy(keys2[HD:P, :, PKEYS:2 * PKEYS], tp[HD:P, :, :]).then_inc(cache_copied, 1)
                    for i in range(2):
                        v.wait_ge(x_loaded, 16 * (i + 1))
                        if i:
                            v.wait_ge(stored, 32)
                            v.wait_ge(qk_turned, 1)
                        v.wait_ge(sq_done, i + 1)
                        chain.do(v.tensor_scalar(rstd[:, :], ss[:, :], 1.0 / D, EPS, ALU.mult, ALU.add))
                        v.tensor_scalar(ss[:, :], rstd[:, :], 1.0, None, ALU.mult).then_inc(rms_ready, 1)
                        v.wait_ge(rms2_ready, i + 1)
                        chain.do(v.reciprocal(rstd[:, :], ss[:, :]))
                        v.tensor_scalar(xn[:, :], x[:, :], rstd[:, 0:1], None, ALU.mult).then_inc(xn_ready, 1)
                        v.wait_ge(turned, i + 1)
                        v.tensor_tensor(hT[:, :, :], tp[:, :, :], g_mem[:, :].unsqueeze(2).to_broadcast([P, KB, P]),
                                        ALU.mult).then_inc(hT_ready, 1)
                        v.wait_ge(gemm_done, i + 1)
                        chain.do(v.tensor_copy(mv[:, i, :], g[0][:, MW:2 * MW]))
                        chain.do(v.tensor_copy(xn[:, MW:2 * MW], g[0][:, 0:MW]))
                        chain.do(v.tensor_tensor(xn[:, 0:MW], xn[:, MW:2 * MW], xn[:, MW:2 * MW], ALU.mult))
                        chain.do(v.tensor_reduce(hss[:, 0:MH], xn[:, 0:MW].rearrange("p (h d) -> p h d", d=HD), AX, ALU.add))
                        v.tensor_scalar(hss[:, 0:MH], hss[:, 0:MH], 1.0 / HD, EPS, ALU.mult, ALU.add).then_inc(qk_squares, 1)
                        v.wait_ge(qk_rms, i + 1)
                        chain.do(v.reciprocal(hrs[:, 0:MH], hss[:, 0:MH]))
                        chain.do(v.tensor_tensor(xn[:, 0:MW].rearrange("p (h d) -> p h d", d=HD), xn[:, MW:2 * MW].rearrange("p (h d) -> p h d", d=HD),
                                                 hrs[:, 0:MH].unsqueeze(2).to_broadcast([P, MH, HD]), ALU.mult))
                        v.tensor_tensor(xn[:, 0:MW].rearrange("p (h d) -> p h d", d=HD), xn[:, 0:MW].rearrange("p (h d) -> p h d", d=HD),
                                        g_km[:, :].unsqueeze(1).to_broadcast([P, MH, HD]), ALU.mult).then_inc(qkn_ready, 1)
                        v.wait_ge(qk_turned, i + 1)
                        v.tensor_copy(mkT[:, :, i * P:(i + 1) * P], tp[:, 0:2, :]).then_inc(kT_ready, 1)

                @block.scalar
                def _(act_):
                    for i in range(2):
                        act_.wait_ge(x_loaded, 16 * (i + 1))
                        if i:
                            act_.wait_ge(xn_ready, 1)
                        act_.activation(pr[:, :], x[:, :], ACT.Square, accum_out=ss[:, :]).then_inc(sq_done, 1)
                        act_.wait_ge(rms_ready, i + 1)
                        act_.activation(ss[:, :], ss[:, :], ACT.Sqrt).then_inc(rms2_ready, 1)
                        act_.wait_ge(qk_squares, i + 1)
                        act_.activation(hss[:, 0:MH], hss[:, 0:MH], ACT.Sqrt).then_inc(qk_rms, 1)

                @block.tensor
                def _(pe):
                    pe.wait_ge(const_made, 1)
                    pe.wait_ge(cache_loaded, 16)
                    for h in range(PH):
                        last = pe.transpose(tp[:, h, :], z[:, h * P:(h + 1) * P], ident[:, :])
                    last.then_inc(cache_turned, 1)
                    for i in range(2):
                        if i == 0:
                            pe.wait_ge(cache_copied, 2)
                        else:
                            pe.wait_ge(kT_ready, i)
                        pe.wait_ge(xn_ready, i + 1)
                        for k in range(KB):
                            last = pe.transpose(tp[:, k, :], xn[:, k * P:(k + 1) * P], ident[:, :])
                        last.then_inc(turned, 1)
                        pe.wait_ge(hT_ready, i + 1)
                        pe.wait_ge(mm_loaded, 32)
                        for k in range(KB):
                            last = pe.matmul(g[0][:, :], hT[:, k, :], wbuf[:, 0, k, :], start=k == 0, stop=k == KB - 1)
                        last.then_inc(gemm_done, 1)
                        pe.wait_ge(qkn_ready, i + 1)
                        for k in range(2):
                            last = pe.transpose(tp[:, k, :], xn[:, k * P:(k + 1) * P], ident[:, :])
                        last.then_inc(qk_turned, 1)
            end_block()


        def heads_of(ap, n):
            return ap.rearrange("p (h d) -> p h d", h=n)

        def prepare_sync(sp, c):
            R = c.rows
            sp.dma_start(x[:R, :], c.x_in).then_inc(x_loaded, 16)
            if c.sample:
                sp.dma_start(v_all[:, 0:2, :], d_cache_a_v[0][0].rearrange("(b p) h d -> p b (h d)", p=P)).then_inc(cache_loaded, 16)
                sp.dma_start(mv[:, :, :], d_cache_m_v[0][0].rearrange("(b p) h d -> p b (h d)", p=P)).then_inc(cache_loaded, 16)
                for b in range(2):
                    sp.dma_start(logf[:, b, :], d_cache_a_logf[0][0][b * P:(b + 1) * P, :]).then_inc(cache_loaded, 16)
                    sp.dma_start(z[:, b * AW:(b + 1) * AW], d_cache_a_k[0][0][b * P:(b + 1) * P].rearrange("p h d -> p (h d)")).then_inc(cache_loaded, 16)
                    sp.dma_start(xn[:, b * MW:(b + 1) * MW], d_cache_m_k[0][0][b * P:(b + 1) * P].rearrange("p h d -> p (h d)")).then_inc(cache_loaded, 16)
                    with nc.allow_non_contiguous_dma("2 rows of history, channels to partitions"):
                        sp.dma_start(uT[:, b, 0:2], d_cache_b_conv[0][0][:, b * P:(b + 1) * P].rearrange("t c -> c t")).then_inc(cache_loaded, 16)
            w_in, w_out, w_pq = d_w_in[0], d_w_out[0], d_w_peer_q[0]
            chunks = ([w_in[:, i * CHUNK:(i + 1) * CHUNK] for i in range(3)] + [w_in[:, BCOL + i * CHUNK:BCOL + (i + 1) * CHUNK] for i in range(2)]
                      + [w_out[:, i * CHUNK:(i + 1) * CHUNK] for i in range(2)] + [w_pq[:, i * CHUNK:(i + 1) * CHUNK] for i in range(2)])
            part = ["norm", "turn", "q", "k", "v", "bc", "hm", "att4", "out0"]
            for n in range(7):
                yield part[n]
                load_chunk(sp, n, [chunks[n]], gemm_done)
            yield "qknorm"
            sp.wait_ge(z_ready, 3)
            sp.dma_start(c.v_out, z[:R, 2 * AW:3 * AW]).then_inc(stored, 16)
            sp.wait_ge(qkn_ready, 2)
            sp.dma_start(c.k_out, z[:R, AW:2 * AW]).then_inc(stored, 16)
            sp.wait_ge(logf_ready, 1)
            sp.dma_start(c.logf_out, lf[:R, 0, :]).then_inc(stored, 16)
            sp.wait_ge(u_ready, 1)
            for b in range(2):
                with nc.allow_non_contiguous_dma("2 rows of convolution state, channels on partitions"):
                    sp.dma_start(c.conv_out[:, b * P:(b + 1) * P].rearrange("t c -> c t"), uT[:, b, R:R + 2]).then_inc(stored, 16)
            for n in (7, 8):
                yield ["out0", "out1"][n - 7]
                load_chunk(sp, n, [chunks[n]], gemm_done)
            yield "top8"
            sp.wait_ge(stored, 16 * 5)

        def prepare_tensor(pe, c):
            R, W = c.rows, c.blocks * P

            def gemm(n, out, lhs, rhs, last_of_chunk=True):
                for k in range(KB):
                    last = pe.matmul(out, lhs(k), rhs(k), start=k == 0, stop=k == KB - 1)
                if last_of_chunk:
                    last.then_inc(gemm_done, 1)

            def chunk_here(n):
                pe.wait_ge(w_loaded[n % 2], 16 * (n // 2 + 1))

            yield "norm"
            if c.sample:
                pe.wait_ge(cache_loaded, 16 * 10)
                for b in range(2):
                    if b:
                        pe.wait_ge(cache_copied, 1)
                    for k in range(4):
                        pe.transpose(tp[:, k, :], z[:, b * AW + k * P:b * AW + (k + 1) * P], ident[:, :])
                    for k in range(2):
                        last = pe.transpose(tp[:, 4 + k, :], xn[:, b * MW + k * P:b * MW + (k + 1) * P], ident[:, :])
                    last.then_inc(cache_turned, 1)
                for b in range(2):
                    if b:
                        pe.wait_ge(ft_used, 1)
                    pe.matmul(g[0][0:AH, 0:P], logf[:, b, :], upto[:, :], start=True, stop=True).then_inc(ft_done, 1)
                pe.wait_ge(cache_copied, 2)
                pe.wait_ge(ft_used, 2)
            yield "turn"
            pe.wait_ge(xn_ready, 1)
            for k in range(KB):
                last = pe.transpose(tp[:, k, :R], xn[:R, k * P:(k + 1) * P], ident[:R, :R])
            last.then_inc(turned, 1)
            pe.wait_ge(hT_ready, 1)
            for k in range(KB):
                last = pe.matmul(tp[:R, 0, 0:AH], hT[:, k, :R], w_f[:, k, :], start=k == 0, stop=k == KB - 1)
            last.then_inc(fl_done, 1)
            for n, name in enumerate("qkv"):
                yield name
                chunk_here(n)
                if n == 2:
                    pe.wait_ge(z_ready, 1)
                gemm(n, g[n % 2][:R, :], lambda k: hT[:, k, :R], lambda k: wbuf[:, n % 2, k, :])
            yield "bc"
            chunk_here(3)
            pe.wait_ge(z_ready, 2)
            for j in range(4):
                gemm(3, g[1][:, j * P:j * P + R], lambda k: wbuf[:, 1, k, j * P:(j + 1) * P], lambda k: hT[:, k, :R], j == 3)
            yield "hm"
            chunk_here(4)
            pe.wait_ge(z_ready, 3)
            for j in range(2):
                gemm(4, g[0][:, j * P:j * P + R], lambda k: wbuf[:, 0, k, j * P:(j + 1) * P], lambda k: hT[:, k, :R], False)
            gemm(4, g[0][:R, MW:2 * MW], lambda k: hT[:, k, :R], lambda k: wbuf[:, 0, k, MW:2 * MW])
            yield "turnqk"
            pe.wait_ge(f_ready, 1)
            pe.wait_ge(qkn_ready, 3)
            for k in range(2 * AW // P):
                last = pe.transpose(tp[:, k, :R], z[:R, k * P:(k + 1) * P], ident[:R, :R])
            last.then_inc(qk_turned, 1)
            pe.wait_ge(qT_ready, 2)
            for k in range(2):
                last = pe.transpose(tp[:, k, :R], z[:R, 3 * AW + k * P:3 * AW + (k + 1) * P], ident[:R, :R])
            last.then_inc(qm_turned, 1)
            pe.wait_ge(logf_ready, 1)
            pe.wait_ge(bcT_ready, 1)
            pe.matmul(g[1][0:AH, 0:R], lf[:R, 0, :], upto[:R, :R], start=True, stop=True).then_inc(cum_done, 1)

            def scores(n):
                if n:
                    pe.wait_ge(exp_done, n)
                if n < AH:
                    for lo in range(0, W, CHUNK):
                        hi = min(lo + CHUNK, W)
                        pe.matmul(S[:R, lo:hi], qT[:, n, :R], kT[:, n // 2, lo:hi], start=True, stop=False)
                    pe.matmul(c.own_keys(S)[:R], ident[:R, :R], causal[:R, :R], start=False, stop=False)
                    for lo in range(0, W, CHUNK):
                        hi = min(lo + CHUNK, W)
                        last = pe.matmul(S[:R, lo:hi], headrow[:, n, :R], negF[:, lo:hi], start=False, stop=True)
                else:
                    last = pe.matmul(S[:R, 0:NMEM], qT[:, n, :R], mkT[:, (n - AH) // 2, :], start=True, stop=True)
                last.then_inc(s_done, 1)

            def blocks(n):
                return c.blocks if n < AH else NMEM // P

            pe.wait_ge(kT_ready, 1)
            pe.wait_ge(qmT_ready, 2)
            pe.wait_ge(cum_used, 1)
            for n in range(UNITS + 1):
                yield f"att{n}"
                if n == 0:
                    scores(0)
                    continue
                m = n - 1
                pe.wait_ge(exp_done, n)
                if m:
                    pe.wait_ge(pT_low, m)
                    pe.wait_ge(pT_high, m)
                for b in range(blocks(m)):
                    last = pe.transpose(tp[:, b, :R], pr[:R, b * P:(b + 1) * P], ident[:R, :R])
                last.then_inc(p_turned, 1)
                if n < UNITS:
                    scores(n)
                pe.wait_ge(pT_low, n)
                pe.wait_ge(pT_high, n)
                for b in range(blocks(m)):
                    if m < AH:
                        out, val = g[0][:R, m * HD:(m + 1) * HD], v_all[:, b, m * HD:(m + 1) * HD]
                    else:
                        out, val = g[1][:R, (m - AH) * HD:(m - AH + 1) * HD], mv[:, b, (m - AH) * HD:(m - AH + 1) * HD]
                    last = pe.matmul(out, pT[:, b, :R], val, start=b == 0, stop=b == blocks(m) - 1)
                last.then_inc(pv_done, 1)
            yield "mix"
            pe.wait_ge(mix_ready, 2)
            for k in range(6):
                last = pe.transpose(tp[:, k, :R], xn[:R, k * P:(k + 1) * P], ident[:R, :R])
            last.then_inc(mix_turned, 1)
            pe.wait_ge(mixT_ready, 2)
            pe.wait_ge(conv_ready, 2)
            for i in range(2):
                yield f"out{i}"
                chunk_here(5 + i)
                gemm(5 + i, S[:R, i * CHUNK:(i + 1) * CHUNK], lambda k: mixT[:, k, :R], lambda k: wbuf[:, (5 + i) % 2, k, :])
            yield "turn2"
            pe.wait_ge(xt_ready, 1)
            for k in range(KB):
                last = pe.transpose(tp[:, k, :R], xtn[:R, k * P:(k + 1) * P], ident[:R, :R])
            last.then_inc(xt_turned, 1)
            pe.wait_ge(xtT_ready, 2)
            for i in range(2):
                yield f"pq{i}"
                chunk_here(7 + i)
                for j in range(4):
                    gemm(7 + i, g[i][:, j * P:j * P + R], lambda k: wbuf[:, (7 + i) % 2, k, j * P:(j + 1) * P], lambda k: hT[:, k, :R], j == 3)
            for h in range(PH):
                yield f"top{h}"
                pe.wait_ge(pqT_ready, h // 4 + 1)
                if h >= 2:
                    pe.wait_ge(picked, h - 1)
                pe.matmul(S[:R, (h % 2) * CHUNK:(h % 2) * CHUNK + 2 * PKEYS], pT[:, h, :R], keys2[:, h, :], start=True, stop=True).then_inc(key_scores, 1)

        def prepare_scalar(sc_, c):
            R, W = c.rows, c.blocks * P
            yield "norm"
            sc_.wait_ge(x_loaded, 16)
            sc_.activation(pr[:R, :], x[:R, :], ACT.Square, accum_out=ss[:R, :]).then_inc(sq_done, 1)
            sc_.wait_ge(rms_ready, 1)
            sc_.activation(ss[:R, :], ss[:R, :], ACT.Sqrt).then_inc(rms_ready, 1)
            for n, name in enumerate("qkv"):
                yield name
                sc_.wait_ge(gemm_done, n + 1)
                if c.sample:
                    sc_.wait_ge(cache_turned, 2)
                sc_.activation(z[:R, n * AW:(n + 1) * AW], g[n % 2][:R, :], ACT.Copy).then_inc(z_ready, 1)
            yield "bc"
            sc_.wait_ge(gemm_done, 4)
            sc_.activation(bcT[:, :, :R], g[1][:, :].rearrange("p (j q) -> p j q", j=4)[:, :, :R], ACT.Copy).then_inc(bcT_ready, 1)
            yield "hm"
            sc_.wait_ge(gemm_done, 5)
            sc_.activation(z[:R, 3 * AW:3 * AW + MW], g[0][:R, MW:2 * MW], ACT.Copy).then_inc(z_ready, 1)
            yield "qknorm"
            sc_.wait_ge(qk_squares, 1)
            sc_.activation(hss[:R, :], hss[:R, :], ACT.Sqrt).then_inc(qk_rms, 1)
            sc_.wait_ge(f_ready, 1)
            sc_.activation(lf[:R, 2, :], lf[:R, 1, :], ACT.Exp).then_inc(f_exp, 1)
            sc_.wait_ge(f_exp, 1)
            sc_.activation(lf[:R, 3, :], lf[:R, 2, :], ACT.Ln, bias=1.0).then_inc(f_ln, 1)
            yield "turnqk"
            sc_.wait_ge(z_ready, 3)
            sc_.activation(c.own_values, z[:R, 2 * AW:3 * AW], ACT.Copy).then_inc(kT_ready, 1)
            sc_.wait_ge(kT_ready, 1)
            for n in range(UNITS + 1):
                yield f"att{n}"
                if n:
                    m = n - 1
                    nb = c.blocks if m < AH else NMEM // P
                    sc_.wait_ge(p_turned, n)
                    if m:
                        sc_.wait_ge(pv_done, m)
                    half = min(nb, 4)
                    if nb > half:
                        sc_.activation(pT[:, half:nb, :R], tp[:, half:nb, :R], ACT.Copy).then_inc(pT_high, 1)
                    else:
                        sc_.sem_inc(pT_high, 1)
                if n < UNITS:
                    w = W if n < AH else NMEM
                    sc_.wait_ge(nmax_ready, n + 1)
                    if n:
                        sc_.wait_ge(p_turned, n)
                    sc_.activation(pr[:R, 0:w], S[:R, 0:w], ACT.Exp, bias=nmax[:R, n:n + 1], accum_out=rsum[:R, n:n + 1]).then_inc(exp_done, 1)
            yield "mix"
            sc_.wait_ge(mix_turned, 1)
            sc_.activation(mixT[:, 0:4, :R], tp[:, 0:4, :R], ACT.Copy).then_inc(mixT_ready, 1)
            sc_.activation(mixT[:, 6:8, :R], tp[:, 4:6, :R], ACT.Copy).then_inc(mixT_ready, 1)
            yield "norm2"
            sc_.wait_ge(x2_ready, 1)
            sc_.activation(pr[:R, :], x2n[:R, :], ACT.Square, accum_out=ss[:R, :]).then_inc(sq2_done, 1)
            sc_.wait_ge(rms2_ready, 1)
            sc_.activation(ss[:R, :], ss[:R, :], ACT.Sqrt).then_inc(rms2_ready, 1)
            yield "turn2"
            sc_.wait_ge(xt_turned, 1)
            for i in range(2):
                sc_.activation(hT[:, 4 * i:4 * i + 4, :R], tp[:, 4 * i:4 * i + 4, :R], ACT.Copy).then_inc(xtT_ready, 1)
            for i in range(2):
                yield f"pq{i}"
                sc_.wait_ge(gemm_done, 8 + i)
                sc_.activation(pT[:, 4 * i:4 * i + 4, :R], g[i][:, :].rearrange("p (j q) -> p j q", j=4)[:, :, :R], ACT.Copy).then_inc(pqT_ready, 1)
            yield "top8"
            sc_.wait_ge(diff_ready, 1)
            sc_.activation(ex[:R, :, :], sc[:R, :, :], ACT.Exp).then_inc(ex_ready, 1)

        def prepare_vector(v, c, chain):
            R, W = c.rows, c.blocks * P
            do = chain.do
            yield "norm"
            if c.sample:
                for b in range(2):
                    v.wait_ge(cache_turned, b + 1)
                    do(v.tensor_copy(kT[:, :, b * P:(b + 1) * P], tp[:, 0:4, :]))
                    v.tensor_copy(mkT[:, :, b * P:(b + 1) * P], tp[:, 4:6, :]).then_inc(cache_copied, 1)
                do(v.memset(negF[0:AH, PAST:PAST + P], NEG))
                do(v.memset(ncarry[:, :], 0.0))
                for b in range(2):
                    v.wait_ge(ft_done, b + 1)
                    do(v.tensor_scalar(negF[0:AH, b * P:(b + 1) * P], g[0][0:AH, 0:P], -1.0, ncarry[:, 0:1], ALU.mult, ALU.add))
                    v.tensor_scalar(ncarry[:, :], g[0][0:AH, P - 1:P], -1.0, ncarry[:, 0:1], ALU.mult, ALU.add).then_inc(ft_used, 1)
                    v.wait_ge(ft_used, b + 1)
                v.wait_ge(cache_loaded, 16 * 10)
            v.wait_ge(sq_done, 1)
            v.tensor_scalar(ss[:R, :], ss[:R, :], 1.0 / D, EPS, ALU.mult, ALU.add).then_inc(rms_ready, 1)
            v.wait_ge(rms_ready, 2)
            do(v.reciprocal(rstd[:R, :], ss[:R, :]))
            v.tensor_scalar(xn[:R, :], x[:R, :], rstd[:R, 0:1], None, ALU.mult).then_inc(xn_ready, 1)
            yield "turn"
            v.wait_ge(turned, 1)
            v.tensor_tensor(hT[:, :, :R], tp[:, :, :R], g_attn[:, :].unsqueeze(2).to_broadcast([P, KB, R]), ALU.mult).then_inc(hT_ready, 1)
            v.wait_ge(fl_done, 1)
            do(v.tensor_tensor(lf[:R, 0, :], tp[:R, 0, 0:AH], bias_f[:R, :], ALU.add))
            do(v.tensor_scalar(lf[:R, 1, :], lf[:R, 0, :], -1.0, None, ALU.mult))
            v.tensor_tensor(lf[:R, 1, :], lf[:R, 1, :], lf[:R, 0, :], ALU.min).then_inc(f_ready, 1)
            yield "hm"
            v.wait_ge(gemm_done, 5)
            v.wait_ge(bcT_ready, 1)
            v.wait_ge(z_ready, 4)
            v.tensor_tensor(uT[:, :, 2:2 + R], bcT[:, 2:4, :R], g[0][:, 0:2 * P].rearrange("p (j q) -> p j q", j=2)[:, :, :R], ALU.mult).then_inc(u_ready, 1)
            v.wait_ge(u_ready, 1)
            for b in range(2):
                do(v.tensor_scalar(yT[:, b, :R], uT[:, b, 2:2 + R], conv_w[:, b, 2:3], conv_b[:, b:b + 1], ALU.mult, ALU.add))
                for j in range(2):
                    do(v.scalar_tensor_tensor(yT[:, b, :R], uT[:, b, j:j + R], conv_w[:, b, j:j + 1], yT[:, b, :R], ALU.mult, ALU.add))
                v.tensor_tensor(mixT[:, 4 + b, :R], yT[:, b, :R], bcT[:, b, :R], ALU.mult).then_inc(conv_ready, 1)
            yield "qknorm"
            v.wait_ge(z_ready, 4)
            do(v.tensor_tensor(pr[:R, :], z[:R, 0:2 * AW], z[:R, 0:2 * AW], ALU.mult))
            do(v.tensor_reduce(hss[:R, 0:16], heads_of(pr[:R, :], 16), AX, ALU.add))
            do(v.tensor_tensor(pr[:R, 0:MW], z[:R, 3 * AW:3 * AW + MW], z[:R, 3 * AW:3 * AW + MW], ALU.mult))
            do(v.tensor_reduce(hss[:R, 16:20], heads_of(pr[:R, 0:MW], MH), AX, ALU.add))
            v.tensor_scalar(hss[:R, :], hss[:R, :], 1.0 / HD, EPS, ALU.mult, ALU.add).then_inc(qk_squares, 1)
            v.wait_ge(qk_rms, 1)
            do(v.reciprocal(hrs[:R, :], hss[:R, :]))
            for lo, h0, nh, gain in ((0, 0, AH, g_q), (AW, AH, AH, g_k), (3 * AW, 2 * AH, MH, g_qm)):
                zz = heads_of(z[:R, lo:lo + nh * HD], nh)
                do(v.tensor_tensor(zz, zz, hrs[:R, h0:h0 + nh].unsqueeze(2).to_broadcast([R, nh, HD]), ALU.mult))
                v.tensor_tensor(zz, zz, gain[:R, :].unsqueeze(1).to_broadcast([R, nh, HD]), ALU.mult).then_inc(qkn_ready, 1)
            v.wait_ge(f_ln, 1)
            do(v.tensor_scalar(lf[:R, 0, :], lf[:R, 0, :], 0.0, None, ALU.min))
            v.tensor_tensor(lf[:R, 0, :], lf[:R, 0, :], lf[:R, 3, :], ALU.subtract).then_inc(logf_ready, 1)
            yield "turnqk"
            v.wait_ge(qk_turned, 1)
            v.tensor_copy(qT[0:HD, 0:AH:2, :R], tp[0:HD, 0:4, :R]).then_inc(qT_ready, 1)
            v.tensor_copy(qT[HD:P, 1:AH:2, :R], tp[HD:P, 0:4, :R]).then_inc(qT_ready, 1)
            do(v.tensor_copy(c.own_keysT, tp[:, 4:8, :R]))
            v.wait_ge(qm_turned, 1)
            v.tensor_copy(qT[0:HD, AH:UNITS:2, :R], tp[0:HD, 0:2, :R]).then_inc(qmT_ready, 1)
            v.tensor_copy(qT[HD:P, AH + 1:UNITS:2, :R], tp[HD:P, 0:2, :R]).then_inc(qmT_ready, 1)
            v.wait_ge(cum_done, 1)
            do(v.tensor_scalar(c.own_negF, g[1][0:AH, 0:R], -1.0, ncarry[:, 0:1], ALU.mult, ALU.add))
            v.tensor_scalar(ncarry[:, :], g[1][0:AH, R - 1:R], -1.0, ncarry[:, 0:1], ALU.mult, ALU.add).then_inc(cum_used, 1)
            for n in range(UNITS + 1):
                yield f"att{n}"
                if n:
                    m = n - 1
                    nb = c.blocks if m < AH else NMEM // P
                    v.wait_ge(p_turned, n)
                    if m:
                        v.wait_ge(pv_done, m)
                    v.tensor_copy(pT[:, 0:min(nb, 4), :R], tp[:, 0:min(nb, 4), :R]).then_inc(pT_low, 1)
                if n < UNITS:
                    v.wait_ge(s_done, n + 1)
                    v.tensor_reduce(nmax[:R, n:n + 1], S[:R, 0:W if n < AH else NMEM], AX, ALU.max, negate=True).then_inc(nmax_ready, 1)
            yield "mix"
            v.wait_ge(exp_done, UNITS)
            do(v.reciprocal(rinv[:R, :], rsum[:R, :]))
            v.wait_ge(pv_done, UNITS)
            v.tensor_tensor(heads_of(xn[:R, 0:AW], AH), heads_of(g[0][:R, :], AH), rinv[:R, 0:AH].unsqueeze(2).to_broadcast([R, AH, HD]), ALU.mult).then_inc(mix_ready, 1)
            v.tensor_tensor(heads_of(xn[:R, AW:AW + MW], MH), heads_of(g[1][:R, 0:MW], MH), rinv[:R, AH:UNITS].unsqueeze(2).to_broadcast([R, MH, HD]), ALU.mult).then_inc(mix_ready, 1)
            v.wait_ge(conv_ready, 2)
            v.wait_ge(stored, 16 * 5)
            do(v.tensor_copy(uT[:, :, 0:2], uT[:, :, R:R + 2]))
            yield "norm2"
            v.wait_ge(gemm_done, 7)
            v.wait_ge(copied, 1)
            v.tensor_tensor(x2n[:R, :], S[:R, :], x[:R, :], ALU.add).then_inc(x2_ready, 1)
            v.wait_ge(sq2_done, 1)
            v.tensor_scalar(ss[:R, :], ss[:R, :], 1.0 / D, EPS, ALU.mult, ALU.add).then_inc(rms2_ready, 1)
            v.wait_ge(rms2_ready, 2)
            do(v.reciprocal(rstd[:R, :], ss[:R, :]))
            v.scalar_tensor_tensor(xtn[:R, :], x2n[:R, :], rstd[:R, 0:1], g_ffn[:R, :], ALU.mult, ALU.mult).then_inc(xt_ready, 1)
            for h in range(PH):
                yield f"top{h}"
                v.wait_ge(key_scores, h + 1)
                for q in range(2):
                    ks = S[:R, (h % 2) * CHUNK + q * PKEYS:(h % 2) * CHUNK + (q + 1) * PKEYS]
                    do(v.max(pick[:R, q, 0:8], ks))
                    do(v.max_index(picki[:R, q, 0:8], pick[:R, q, 0:8], ks))
                    ins = v.match_replace(left[:R, q, :], pick[:R, q, 0:8], ks, GONE)
                    if q == 0:
                        do(ins)
                    else:
                        ins.then_inc(picked, 1)
                        v.wait_ge(picked, h + 1)
                    do(v.max(pick[:R, q, 8:16], left[:R, q, :]))
                    do(v.max_index(picki[:R, q, 8:16], pick[:R, q, 8:16], left[:R, q, :]))
                do(v.tensor_tensor(cand[:R, :, :], pick[:R, 0, :].unsqueeze(2).to_broadcast([R, TOPK, TOPK]),
                                   pick[:R, 1, :].unsqueeze(1).to_broadcast([R, TOPK, TOPK]), ALU.add))
                cands = cand[:R, :, :].rearrange("p i j -> p (i j)")
                do(v.max(sc[:R, h, 0:8], cands))
                do(v.max_index(ci[:R, 0:8], sc[:R, h, 0:8], cands))
                do(v.match_replace(candleft[:R, :], sc[:R, h, 0:8], cands, GONE))
                do(v.max(sc[:R, h, 8:16], candleft[:R, :]))
                do(v.max_index(ci[:R, 8:16], sc[:R, h, 8:16], candleft[:R, :]))
                do(v.tensor_scalar(cij[:R, 0, :], ci[:R, :], 4, None, ALU.logical_shift_right))
                do(v.tensor_scalar(cij[:R, 1, :], ci[:R, :], TOPK - 1, None, ALU.bitwise_and))
                do(v.tensor_copy(cijf[:R, :, :], cij[:R, :, :]))
                do(v.tensor_copy(pickf[:R, :, :], picki[:R, :, :]))
                for q in range(2):
                    do(v.tensor_tensor(onehot[:R, q], iota16[:R, :].unsqueeze(1).to_broadcast([R, TOPK, TOPK]),
                                       cijf[:R, q, :].unsqueeze(2).to_broadcast([R, TOPK, TOPK]), ALU.is_equal))
                    do(v.tensor_tensor(onehot[:R, q], onehot[:R, q], pickf[:R, q, :].unsqueeze(1).to_broadcast([R, TOPK, TOPK]), ALU.mult))
                    do(v.tensor_reduce(e12[:R, q, :], onehot[:R, q], AX, ALU.add))
                do(v.scalar_tensor_tensor(idxn[:R, h, :], e12[:R, 0, :], float(PKEYS), e12[:R, 1, :], ALU.mult, ALU.add))
            yield "top8"
            v.tensor_tensor(ex[:R, :, :], sc[:R, :, :], sc[:R, :, 0:1].to_broadcast([R, PH, TOPK]), ALU.subtract).then_inc(diff_ready, 1)
            v.wait_ge(ex_ready, 1)
            do(v.tensor_reduce(esum[:R, :], ex[:R, :, :], AX, ALU.add))
            do(v.reciprocal(esum[:R, :], esum[:R, :]))
            do(v.tensor_tensor(gaten[:R, :, :], ex[:R, :, :], esum[:R, :].unsqueeze(2).to_broadcast([R, PH, TOPK]), ALU.mult))


        def experts_gpsimd(pool, e):
            R = e.rows
            pool.wait_ge(copied, 1)
            for n in range(STEPS):
                if n < SLOTS:
                    if n >= NU:
                        pool.wait_ge(dots, n - NU + 1)
                    pool.indirect_dma_start(urow[:R, n % NU, :], None, d_peer_u[0], bass.IndirectOffsetOnAxis(ap=idx[:R, n:n + 1], axis=0)).then_inc(u_landed[n % NU], 16)
                m = n - VLAG + NV // 2
                if 0 <= m < SLOTS:
                    if m >= NV:
                        pool.wait_ge(v_used, m - NV + 1)
                    pool.indirect_dma_start(vrow[:R, m % NV, :], None, d_peer_v[0], bass.IndirectOffsetOnAxis(ap=idx[:R, m:m + 1], axis=0)).then_inc(v_landed[m % NV], 16)
            for i in range(NU):
                pool.wait_ge(u_landed[i], 16 * (SLOTS // NU))
            for i in range(NV):
                pool.wait_ge(v_landed[i], 16 * (SLOTS // NV))
            pool.dma_reset()

        def experts_vector(v, e, chain):
            R = e.rows
            for n in range(STEPS):
                yield n
                if n < SLOTS:
                    v.wait_ge(u_landed[n % NU], 16 * (n // NU + 1))
                    u = urow[:R, n % NU, :]
                    v.tensor_tensor_reduce(u, u, xt[:R, :], 1.0, 0.0, ALU.mult, ALU.add, act[:R, n // TOPK, n % TOPK:n % TOPK + 1]).then_inc(dots, 1)
                if n % TOPK == 4 and TOPK <= n < SLOTS + TOPK:
                    h = n // TOPK - 1
                    v.wait_ge(gelu_done, h + 1)
                    v.tensor_tensor(wgt[:R, h * TOPK:(h + 1) * TOPK], gel[:R, h, :], gate[:R, h, :], ALU.mult).then_inc(wgt_ready, 1)
            v.wait_ge(acc_done, 1)
            v.tensor_tensor(x2[:R, :], x2[:R, :], acc[:R, :], ALU.add).then_inc(y_ready, 1)

        def experts_scalar(sc_, e):
            R = e.rows
            for n in range(STEPS):
                yield n
                if n % TOPK == 2 and TOPK <= n < SLOTS + TOPK:
                    h = n // TOPK - 1
                    sc_.wait_ge(dots, (h + 1) * TOPK)
                    sc_.activation(gel[:R, h, :], act[:R, h, :], ACT.Gelu).then_inc(gelu_done, 1)
                m = n - VLAG + 1
                if 0 <= m < SLOTS:
                    sc_.wait_ge(wgt_ready, m // TOPK + 1)
                    if m >= ND:
                        sc_.wait_ge(v_used, m - ND + 1)
                    sc_.activation(diag[:R, m % ND, :R], ident[:R, :R], ACT.Copy, scale=wgt[:R, m:m + 1]).then_inc(diag_ready, 1)

        def experts_tensor(pe, e):
            R = e.rows
            for n in range(STEPS):
                yield n
                m = n - VLAG
                if m >= 0:
                    pe.wait_ge(diag_ready, m + 1)
                    pe.wait_ge(v_landed[m % NV], 16 * (m // NV + 1))
                    for i in range(2):
                        last = pe.matmul(acc[:R, i * CHUNK:(i + 1) * CHUNK], diag[:R, m % ND, :R], vrow[:R, m % NV, i * CHUNK:(i + 1) * CHUNK],
                                         start=m == 0, stop=m == SLOTS - 1)
                    last.then_inc(v_used, 1)
            pe.wait_ge(v_used, SLOTS)
            pe.sem_inc(acc_done, 1)

        def block_of(e, c):
            def both(experts, prepare):
                beside(experts if experts is not None else [], [prepare, None] if prepare is not None else None)

            with nc.Block() as block:
                @block.sync
                def _(sp):
                    if c is not None:
                        both(None, prepare_sync(sp, c))
                    if e is not None:
                        sp.wait_ge(y_ready, 1)
                        sp.dma_start(e.y_out, x2[:e.rows, :]).then_inc(y_stored, 16)
                        sp.wait_ge(y_stored, 16)

                if e is not None:
                    @block.gpsimd
                    def _(pool):
                        experts_gpsimd(pool, e)

                @block.vector
                def _(v):
                    chain = Chain(v, dve_chain)
                    if e is not None:
                        R = e.rows
                        chain.do(v.tensor_copy(idx[:R, :], idxn[:R, :, :].rearrange("p h k -> p (h k)")))
                        chain.do(v.tensor_copy(gate[:R, :, :], gaten[:R, :, :]))
                        chain.do(v.tensor_copy(x2[:R, :], x2n[:R, :]))
                        v.tensor_copy(xt[:R, :], xtn[:R, :]).then_inc(copied, 1)
                        v.wait_ge(copied, 1)
                    else:
                        v.sem_inc(copied, 1)
                    both(experts_vector(v, e, chain) if e is not None else None, prepare_vector(v, c, chain) if c is not None else None)

                @block.scalar
                def _(sc_):
                    both(experts_scalar(sc_, e) if e is not None else None, prepare_scalar(sc_, c) if c is not None else None)

                @block.tensor
                def _(pe):
                    both(experts_tensor(pe, e) if e is not None else None, prepare_tensor(pe, c) if c is not None else None)
            end_block()

        def prompt_tile(t, blocks):
            rows = bass.ds(t * P, P)
            return NextTile(
                rows=P, blocks=blocks, sample=False, x_in=d_x_prompt[0][rows, :],
                own_keys=lambda m: m[:, rows], own_keysT=kT[:, :, rows], own_negF=negF[0:AH, rows],
                own_values=v_all[:, bass.ds(t, 1), :].rearrange("p a n -> p (a n)"),
                k_out=d_a_k[0][0][rows].rearrange("n h d -> n (h d)"), v_out=d_a_v[0][0][rows].rearrange("n h d -> n (h d)"),
                logf_out=d_a_logf[0][0][rows, :], conv_out=d_b_conv[0][0])

        sample_tile = NextTile(
            rows=NEW, blocks=3, sample=True, x_in=d_x_sample[0],
            own_keys=lambda m: m[:, PAST:PAST + NEW], own_keysT=kT[:, :, PAST:PAST + NEW], own_negF=negF[0:AH, PAST:PAST + NEW],
            own_values=v_all[0:NEW, 2, :],
            k_out=d_a_k_s[0][0].rearrange("n h d -> n (h d)"), v_out=d_a_v_s[0][0].rearrange("n h d -> n (h d)"),
            logf_out=d_a_logf_s[0][0], conv_out=d_b_conv_s[0][0])

        def prompt_experts(t):
            return Tile(rows=P, y_out=d_y_prompt[0][bass.ds(t * P, P), :])

        setup()
        block_of(None, prompt_tile(0, 1))
        for first, last, blocks in ((0, TILES // 2 - 1, TILES // 2), (TILES // 2 - 1, TILES - 1, TILES)):
            with nc.Fori(first, last) as t:
                block_of(prompt_experts(t), prompt_tile(t + 1, blocks))
        block_of(prompt_experts(TILES - 1), sample_tile)
        block_of(Tile(rows=NEW, y_out=d_y_sample[0]), None)


_INS = ['x_prompt', 'x_sample', 'cache_a_k', 'cache_a_v', 'cache_a_logf', 'cache_b_conv', 'cache_m_k', 'cache_m_v',
        'mem_prompt', 'g_attn', 'w_in', 'b_f', 'g_q_a', 'g_k_a', 'conv_w', 'conv_b', 'g_mem', 'w_mem_k', 'w_mem_v',
        'g_k_m', 'g_q_m', 'w_out', 'g_ffn', 'w_peer_q', 'peer_keys', 'peer_u', 'peer_v']
_OUTS = [('y_prompt', (1, 1024, 1024)), ('y_sample', (1, 32, 1024)), ('a_k', (1, 1, 1024, 8, 64)), ('a_v', (1, 1, 1024, 8, 64)),
         ('a_logf', (1, 1, 1024, 8)), ('b_conv', (1, 1, 2, 256)), ('m_k', (1, 1, 256, 4, 64)), ('m_v', (1, 1, 256, 4, 64)),
         ('a_k_s', (1, 1, 32, 8, 64)), ('a_v_s', (1, 1, 32, 8, 64)), ('a_logf_s', (1, 1, 32, 8)), ('b_conv_s', (1, 1, 2, 256))]


def kernel(**inputs):
    import numpy as _np
    import concourse.bacc as _bacc
    from concourse import mybir as _mybir
    from concourse.bass_utils import run_bass_kernel_spmd as _run

    nc = _bacc.Bacc("TRN2", target_bir_lowering=False, num_devices=1)
    arrays, args = {}, []
    for name in _INS:
        v = _np.ascontiguousarray(inputs[name])
        arrays[f"in_{name}_dram"] = v
        args.append(nc.dram_tensor(f"in_{name}_dram", v.shape, _mybir.dt.from_np(v.dtype), kind="ExternalInput").ap())
    for name, shape in _OUTS:
        args.append(nc.dram_tensor(f"out_{name}_dram", shape, F32, kind="ExternalOutput").ap())
    build(nc, *args)
    r = _run(nc, [arrays], core_ids=[0])
    return tuple(r.results[0][f"out_{name}_dram"] for name, _ in _OUTS)
```

```python
from contextlib import ExitStack

import concourse.bass as bass
from concourse import mybir

F32 = mybir.dt.float32
U32 = mybir.dt.uint32
ALU = mybir.AluOpType
ACT = mybir.ActivationFunctionType
AX = mybir.AxisListType.X

P = 128
D = 1024
KB = D // P
SEQ, NEW, PAST, NMEM = 1024, 32, 256, 256
TILES = SEQ // P
AH, MH, HD = 8, 4, 64
AW, BW, MW = AH * HD, 256, MH * HD
FCOL = 3 * AW
BCOL = FCOL + AH
BANK = 512
CHUNK = 256
PH, PKEYS, TOPK = 8, 128, 16
SLOTS = PH * TOPK
NEXP = PKEYS * PKEYS
EPS = 1e-6
NEG = -1e30
GONE = -3e38
UNITS = AH + MH
NU, NV, ND, NW = 7, 7, 4, 4
VLAG = 24
AHEAD = 5
LIGHT = 88


class Tile:

    def __init__(self, tokens, y_out, alone=False):
        self.tokens, self.y_out, self.alone = tokens, y_out, alone
        self.groups = P // tokens
        self.slots = SLOTS // self.groups
        self.steps = self.slots + VLAG
        self.ahead = AHEAD if self.groups == 1 else 0

    def on_vector(self, m):
        return m % 2 == 1 and (self.alone or not LIGHT <= m + VLAG < SLOTS)

    def vector_slots(self, m):
        return sum(self.on_vector(i) for i in range(m + 1))

    def tensor_slots(self, m):
        return m + 1 - self.vector_slots(m)

    def landings(self, n):
        return n // NU + (n % NU >= self.ahead)


class Chain:

    def __init__(self, eng, sem):
        self.eng, self.sem, self.n = eng, sem, 0

    def add(self, ins):
        self.n += 1
        ins.then_inc(self.sem, 1)

    def settle(self):
        self.eng.wait_ge(self.sem, self.n)

    def do(self, ins):
        self.add(ins)
        self.settle()


PARTS = ([("square", 1), ("rms", 1), ("root", 1), ("scale", 1), ("turn", 1), ("hT", 1)]
         + [(f"w{n}", 2) for n in range(10)]
         + [("qm", .5), ("conv", 1), ("headsq", 1.5), ("headroot", .5), ("headnorm", 2), ("turnqk", 1), ("qT", 1), ("turnqm", .5), ("qmT", .5)]
         + [(f"att{n}{x}", 1 if n <= AH else .7) for n in range(UNITS + 1) for x in "abc"]
         + [("mix", 1), ("turnmix", 1), ("mixT", .5)] + [(f"w{n}", 2) for n in range(10, 14)]
         + [("residual", .5), ("square2", .5), ("rms2", .5), ("root2", .5), ("scale2", 1), ("turn2", 1), ("xtT", .5)]
         + [(f"w{n}", 2) for n in range(14, 18)] + [("pqT", .5)]
         + [(f"top{h}", 4.5) for h in range(PH)] + [(f"top{PH}", 1)] + [("gate0", .5), ("gate1", .5), ("gate2", 0)])


def part_steps():
    at, steps, total = 0, {}, sum(w for _, w in PARTS)
    for part, w in PARTS:
        time = at / total * (2 * SLOTS - VLAG)
        steps[part] = int(time if time < VLAG else VLAG + (time - VLAG) / 2)
        at += w
    return steps


AT = part_steps()


def beside(experts, prepare):
    for n in experts:
        while prepare is not None:
            if prepare[1] is None or AT[prepare[1]] <= n:
                prepare[1] = next(prepare[0], False)
                if prepare[1] is False:
                    prepare = None
            else:
                break
    if prepare is not None:
        for _ in prepare[0]:
            pass


class NextTile:

    def __init__(self, rows, blocks, sample, x_in, own_keys, own_keysT, own_negF, own_values, k_out, v_out, logf_out, conv_out):
        self.rows, self.blocks, self.sample, self.x_in = rows, blocks, sample, x_in
        self.own_keys, self.own_keysT, self.own_negF, self.own_values = own_keys, own_keysT, own_negF, own_values
        self.k_out, self.v_out, self.logf_out, self.conv_out = k_out, v_out, logf_out, conv_out


def build(nc, d_x_prompt, d_x_sample, d_cache_a_k, d_cache_a_v, d_cache_a_logf, d_cache_b_conv, d_cache_m_k, d_cache_m_v, d_mem_prompt, d_g_attn, d_w_in, d_b_f, d_g_q_a, d_g_k_a, d_conv_w, d_conv_b, d_g_mem, d_w_mem_k, d_w_mem_v, d_g_k_m, d_g_q_m, d_w_out, d_g_ffn, d_w_peer_q, d_peer_keys, d_peer_u, d_peer_v,
          d_y_prompt, d_y_sample, d_a_k, d_a_v, d_a_logf, d_b_conv, d_m_k, d_m_v, d_a_k_s, d_a_v_s, d_a_logf_s, d_b_conv_s):
    with ExitStack() as ctx:
        def sb(name, shape, dt=F32):
            return ctx.enter_context(nc.sbuf_tensor(name, shape, dt))

        ident = sb("ident", [P, P])
        upto = sb("upto", [P, P])
        causal = sb("causal", [P, P])
        headrow = sb("headrow", [P, AH, P])
        fold = sb("fold", [P, NEW])
        iota16 = sb("iota16", [P, TOPK])
        g_attn = sb("g_attn", [P, KB])
        g_mem = sb("g_mem", [P, KB])
        g_ffn = sb("g_ffn", [P, D])
        g_q = sb("g_q", [P, HD])
        g_k = sb("g_k", [P, HD])
        g_qm = sb("g_qm", [P, HD])
        g_km = sb("g_km", [P, HD])
        bias_f = sb("bias_f", [P, AH])
        conv_w = sb("conv_w", [P, 2, 3])
        conv_b = sb("conv_b", [P, 2])
        w_f = sb("w_f", [P, KB, AH])
        keys2 = sb("keys2", [P, PH, 2 * PKEYS])
        kT = sb("kT", [P, AH // 2, SEQ])
        v_all = sb("v_all", [P, TILES, AW])
        negF = sb("negF", [P, SEQ])
        ncarry = sb("ncarry", [AH, 1])
        mkT = sb("mkT", [P, MH // 2, NMEM])
        mv = sb("mv", [P, NMEM // P, MW])
        wbuf = sb("wbuf", [P, NW, KB, CHUNK])
        x = sb("x", [P, D])
        xn = sb("xn", [P, D])
        hT = sb("hT", [P, KB, P])
        mixT = hT
        z = sb("z", [P, 3 * AW + MW])
        qT = sb("qT", [P, UNITS, P])
        pr = sb("pr", [P, SEQ])
        pT = sb("pT", [P, TILES, P])
        uT = sb("uT", [P, 2, 2 + P])
        bcT = sb("bcT", [P, 4, P])
        yT = sb("yT", [P, 2, P])
        ss = sb("ss", [P, 1])
        rstd = sb("rstd", [P, 1])
        hss = sb("hss", [P, 20])
        hrs = sb("hrs", [P, 20])
        lf = sb("lf", [P, 4, AH])
        logf = sb("logf", [P, 2, AH])
        nmax = sb("nmax", [P, UNITS])
        rsum = sb("rsum", [P, UNITS])
        rinv = sb("rinv", [P, UNITS])
        pick = sb("pick", [P, 2, TOPK])
        picki = sb("picki", [P, 2, TOPK], U32)
        pickf = sb("pickf", [P, 2, TOPK])
        ks = sb("ks", [P, 2, 2 * PKEYS])
        left = sb("left", [P, 2, PKEYS])
        onehot = pr[:, 0:512].rearrange("p (q i j) -> p q i j", q=2, i=TOPK)
        cand = pr[:, 512:768].rearrange("p (i j) -> p i j", i=TOPK)
        candleft = pr[:, 768:1024]
        ci = sb("ci", [P, TOPK], U32)
        cij = sb("cij", [P, 2, TOPK], U32)
        cijf = sb("cijf", [P, 2, TOPK])
        e12 = sb("e12", [P, 2, TOPK])
        sc = sb("sc", [P, PH, TOPK])
        ex = sb("ex", [P, PH, TOPK])
        esum = sb("esum", [P, PH])
        x2n, xtn = x, xn
        idxn = sb("idxn", [P, PH, TOPK], U32)
        gaten = sb("gaten", [P, PH, TOPK])
        xt = sb("xt", [P, D])
        idx = sb("idx", [P, SLOTS], U32)
        gate = sb("gate", [P, PH, TOPK])
        urow = sb("urow", [P, NU, D])
        vrow = sb("vrow", [P, NV, D])
        act = sb("act", [P, PH, TOPK])
        gel = sb("gel", [P, PH, TOPK])
        wgt = sb("wgt", [P, SLOTS])
        diag = sb("diag", [P, ND, P])
        acc2 = sb("acc2", [P, D])

        def ps(name, shape):
            return ctx.enter_context(nc.psum_tensor(name, shape, F32))

        acc = ps("acc", [P, D])
        S = ps("S", [P, SEQ])
        tp = ps("tp", [P, KB, P])
        g = [ps("g0", [P, BANK]), ps("g1", [P, BANK])]

        def sem(name):
            return ctx.enter_context(nc.semaphore(name))

        const_loaded = sem("const_loaded")
        const_made = sem("const_made")
        zeroed = sem("zeroed")
        gains = sem("gains")
        x_loaded = sem("x_loaded")
        xn_ready = sem("xn_ready")
        sq_done = sem("sq_done")
        rms_ready = sem("rms_ready")
        turned = sem("turned")
        hT_ready = sem("hT_ready")
        fl_done = sem("fl_done")
        gemm_done = sem("gemm_done")
        z_ready = sem("z_ready")
        bcT_ready = sem("bcT_ready")
        qk_squares = sem("qk_squares")
        qk_rms = sem("qk_rms")
        qkn_ready = sem("qkn_ready")
        qk_turned = sem("qk_turned")
        qT_ready = sem("qT_ready")
        kT_ready = sem("kT_ready")
        qm_turned = sem("qm_turned")
        qmT_ready = sem("qmT_ready")
        f_ready = sem("f_ready")
        f_exp = sem("f_exp")
        f_ln = sem("f_ln")
        logf_ready = sem("logf_ready")
        cum_done = sem("cum_done")
        cum_used = sem("cum_used")
        s_done = sem("s_done")
        nmax_ready = sem("nmax_ready")
        exp_done = sem("exp_done")
        p_turned = sem("p_turned")
        pT_ready = sem("pT_ready")
        v_added = sem("v_added")
        pv_done = sem("pv_done")
        mix_ready = sem("mix_ready")
        mix_turned = sem("mix_turned")
        mixT_ready = sem("mixT_ready")
        u_ready = sem("u_ready")
        conv_ready = sem("conv_ready")
        x2_ready = sem("x2_ready")
        sq2_done = sem("sq2_done")
        rms2_ready = sem("rms2_ready")
        xt_ready = sem("xt_ready")
        xt_turned = sem("xt_turned")
        xtT_ready = sem("xtT_ready")
        pqT_ready = sem("pqT_ready")
        key_scores = sem("key_scores")
        picked = sem("picked")
        ks_ready = sem("ks_ready")
        diff_ready = sem("diff_ready")
        ex_ready = sem("ex_ready")
        stored = sem("stored")
        first_picked = sem("first_picked")
        copied = sem("copied")
        idx_spread = sem("idx_spread")
        xt_spread = sem("xt_spread")
        gate_spread = sem("gate_spread")
        acc2_zeroed = sem("acc2_zeroed")
        x2_copied = sem("x2_copied")
        dots = sem("dots")
        gelu_done = sem("gelu_done")
        wgt_ready = sem("wgt_ready")
        diag_ready = sem("diag_ready")
        v_used = sem("v_used")
        y_ready = sem("y_ready")
        y_stored = sem("y_stored")
        dve_chain = sem("dve_chain")
        pool_chain = sem("pool_chain")
        cache_loaded = sem("cache_loaded")
        cache_turned = sem("cache_turned")
        cache_copied = sem("cache_copied")
        ft_done = sem("ft_done")
        ft_used = sem("ft_used")
        mm_loaded = sem("mm_loaded")
        w_loaded = [sem(f"w_loaded{i}") for i in range(NW)]
        u_landed = [sem(f"u_landed{i}") for i in range(NU)]
        v_landed = [sem(f"v_landed{i}") for i in range(NV)]
        first, last = const_loaded.num, v_landed[NV - 1].num
        every_semaphore = range(first, last + 1)
        assert len(every_semaphore) == 75 + NW + NU + NV

        def end_block():
            nc.all_engine_barrier(sems_to_clear=every_semaphore)

        def load_chunk(sp, n, src):
            if n >= NW:
                sp.wait_ge(gemm_done, n - NW + 1)
            sp.dma_start(wbuf[:, n % NW, :, :], src.rearrange("(k p) n -> p k n", p=P)).then_inc(w_loaded[n % NW], 16)

        def setup():
            with nc.Block() as block:
                @block.sync
                def _(sp):
                    loads = [(g_attn[:, :], d_g_attn[0].rearrange("(k p) -> p k", p=P)),
                             (g_mem[:, :], d_g_mem[0].rearrange("(k p) -> p k", p=P)),
                             (g_ffn[:, :], d_g_ffn[0].partition_broadcast(P)),
                             (g_q[:, :], d_g_q_a[0].partition_broadcast(P)),
                             (g_k[:, :], d_g_k_a[0].partition_broadcast(P)),
                             (g_qm[:, :], d_g_q_m[0].partition_broadcast(P)),
                             (g_km[:, :], d_g_k_m[0].partition_broadcast(P)),
                             (bias_f[:, :], d_b_f[0].partition_broadcast(P)),
                             (w_f[:, :, :], d_w_in[0][:, FCOL:BCOL].rearrange("(k p) n -> p k n", p=P))]
                    for j in range(3):
                        loads.append((conv_w[:, :, j], d_conv_w[0][j].rearrange("(b p) -> p b", p=P)))
                    loads.append((conv_b[:, :], d_conv_b[0].rearrange("(b p) -> p b", p=P)))
                    with nc.allow_non_contiguous_dma("vectors laid along partitions, once"):
                        for dst, src in loads:
                            sp.dma_start(dst, src).then_inc(const_loaded, 16)
                    sp.dma_start(wbuf[:, 0, :, 0:MW], d_w_mem_k[0].rearrange("(k p) n -> p k n", p=P)).then_inc(mm_loaded, 16)
                    sp.dma_start(wbuf[:, 1, :, :], d_w_mem_v[0].rearrange("(k p) n -> p k n", p=P)).then_inc(mm_loaded, 16)
                    sp.dma_start(z[:, 0:D].rearrange("p (g d) -> p g d", d=HD),
                                 d_peer_keys[0].rearrange("h q k d -> k (h q) d")).then_inc(cache_loaded, 16)
                    for i in range(2):
                        if i:
                            sp.wait_ge(xn_ready, 1)
                        sp.dma_start(x[:, :], d_mem_prompt[0][i * P:(i + 1) * P, :]).then_inc(x_loaded, 16)
                        sp.wait_ge(qkn_ready, i + 1)
                        sp.dma_start(d_m_k[0][0][i * P:(i + 1) * P].rearrange("n h d -> n (h d)"), xn[:, 0:MW]).then_inc(stored, 16)
                        sp.dma_start(d_m_v[0][0][i * P:(i + 1) * P].rearrange("n h d -> n (h d)"), mv[:, i, :]).then_inc(stored, 16)
                    sp.wait_ge(stored, 64)
                    sp.wait_ge(const_loaded, 16 * len(loads))

                @block.gpsimd
                def _(pool):
                    chain = Chain(pool, pool_chain)
                    chain.do(pool.memset(ident[:, :], 0.0))
                    chain.do(pool.affine_select(ident[:, :], ident[:, :], [[-1, P]], ALU.not_equal, 1.0, base=0, channel_multiplier=1))
                    chain.do(pool.memset(upto[:, :], 1.0))
                    chain.do(pool.affine_select(upto[:, :], upto[:, :], [[1, P]], ALU.is_ge, 0.0, base=0, channel_multiplier=-1))
                    chain.do(pool.memset(causal[:, :], 0.0))
                    chain.do(pool.affine_select(causal[:, :], causal[:, :], [[-1, P]], ALU.is_ge, NEG, base=0, channel_multiplier=1))
                    chain.do(pool.memset(headrow[:, :, :], 0.0))
                    chain.do(pool.affine_select(headrow[:, :, :], headrow[:, :, :], [[-1, AH], [0, P]], ALU.not_equal, 1.0, base=0, channel_multiplier=1))
                    chain.do(pool.tensor_copy(fold[:, :], ident[:, 0:NEW]))
                    for i in range(1, P // NEW):
                        chain.do(pool.tensor_tensor(fold[:, :], fold[:, :], ident[:, i * NEW:(i + 1) * NEW], ALU.add))
                    pool.iota(iota16[:, :], [[1, TOPK]], base=0, channel_multiplier=0,
                              allow_small_or_imprecise_dtypes=True).then_inc(const_made, 1)

                @block.vector
                def _(v):
                    chain = Chain(v, dve_chain)
                    v.memset(kT[:, :, :], 0.0).then_inc(zeroed, 1)
                    v.memset(v_all[:, :, :], 0.0).then_inc(zeroed, 1)
                    chain.do(v.memset(negF[:, :], 0.0))
                    v.memset(negF[0:AH, :], NEG).then_inc(zeroed, 1)
                    v.memset(ncarry[:, :], 0.0).then_inc(zeroed, 1)
                    v.memset(qT[:, :, :], 0.0).then_inc(zeroed, 1)
                    v.memset(uT[:, :, :], 0.0).then_inc(zeroed, 1)
                    chain.do(v.memset(keys2[:, :, :], 0.0))
                    v.wait_ge(const_loaded, 16 * 13)
                    v.tensor_scalar(g_q[:, :], g_q[:, :], HD ** -0.5, None, ALU.mult).then_inc(gains, 1)
                    v.tensor_scalar(g_qm[:, :], g_qm[:, :], HD ** -0.5, None, ALU.mult).then_inc(gains, 1)
                    v.wait_ge(cache_turned, 1)
                    v.tensor_copy(keys2[0:HD, :, 0:PKEYS], tp[0:HD, :, :]).then_inc(cache_copied, 1)
                    v.tensor_copy(keys2[HD:P, :, PKEYS:2 * PKEYS], tp[HD:P, :, :]).then_inc(cache_copied, 1)
                    for i in range(2):
                        v.wait_ge(x_loaded, 16 * (i + 1))
                        if i:
                            v.wait_ge(stored, 32)
                            v.wait_ge(qk_turned, 1)
                        v.wait_ge(sq_done, i + 1)
                        chain.do(v.tensor_scalar(rstd[:, :], ss[:, :], 1.0 / D, EPS, ALU.mult, ALU.add))
                        v.tensor_scalar(ss[:, :], rstd[:, :], 1.0, None, ALU.mult).then_inc(rms_ready, 1)
                        v.wait_ge(rms2_ready, i + 1)
                        chain.do(v.reciprocal(rstd[:, :], ss[:, :]))
                        v.tensor_scalar(xn[:, :], x[:, :], rstd[:, 0:1], None, ALU.mult).then_inc(xn_ready, 1)
                        v.wait_ge(turned, i + 1)
                        v.tensor_tensor(hT[:, :, :], tp[:, :, :], g_mem[:, :].unsqueeze(2).to_broadcast([P, KB, P]),
                                        ALU.mult).then_inc(hT_ready, 1)
                        v.wait_ge(gemm_done, i + 1)
                        chain.do(v.tensor_copy(mv[:, i, :], g[0][:, MW:2 * MW]))
                        chain.do(v.tensor_copy(xn[:, MW:2 * MW], g[0][:, 0:MW]))
                        chain.do(v.tensor_tensor(xn[:, 0:MW], xn[:, MW:2 * MW], xn[:, MW:2 * MW], ALU.mult))
                        chain.do(v.tensor_reduce(hss[:, 0:MH], xn[:, 0:MW].rearrange("p (h d) -> p h d", d=HD), AX, ALU.add))
                        v.tensor_scalar(hss[:, 0:MH], hss[:, 0:MH], 1.0 / HD, EPS, ALU.mult, ALU.add).then_inc(qk_squares, 1)
                        v.wait_ge(qk_rms, i + 1)
                        chain.do(v.reciprocal(hrs[:, 0:MH], hss[:, 0:MH]))
                        chain.do(v.tensor_tensor(xn[:, 0:MW].rearrange("p (h d) -> p h d", d=HD), xn[:, MW:2 * MW].rearrange("p (h d) -> p h d", d=HD),
                                                 hrs[:, 0:MH].unsqueeze(2).to_broadcast([P, MH, HD]), ALU.mult))
                        v.tensor_tensor(xn[:, 0:MW].rearrange("p (h d) -> p h d", d=HD), xn[:, 0:MW].rearrange("p (h d) -> p h d", d=HD),
                                        g_km[:, :].unsqueeze(1).to_broadcast([P, MH, HD]), ALU.mult).then_inc(qkn_ready, 1)
                        v.wait_ge(qk_turned, i + 1)
                        v.tensor_copy(mkT[:, :, i * P:(i + 1) * P], tp[:, 0:2, :]).then_inc(kT_ready, 1)

                @block.scalar
                def _(act_):
                    for i in range(2):
                        act_.wait_ge(x_loaded, 16 * (i + 1))
                        if i:
                            act_.wait_ge(xn_ready, 1)
                        act_.activation(pr[:, :], x[:, :], ACT.Square, accum_out=ss[:, :]).then_inc(sq_done, 1)
                        act_.wait_ge(rms_ready, i + 1)
                        act_.activation(ss[:, :], ss[:, :], ACT.Sqrt).then_inc(rms2_ready, 1)
                        act_.wait_ge(qk_squares, i + 1)
                        act_.activation(hss[:, 0:MH], hss[:, 0:MH], ACT.Sqrt).then_inc(qk_rms, 1)

                @block.tensor
                def _(pe):
                    pe.wait_ge(const_made, 1)
                    pe.wait_ge(cache_loaded, 16)
                    for h in range(PH):
                        last = pe.transpose(tp[:, h, :], z[:, h * P:(h + 1) * P], ident[:, :])
                    last.then_inc(cache_turned, 1)
                    for i in range(2):
                        if i == 0:
                            pe.wait_ge(cache_copied, 2)
                        else:
                            pe.wait_ge(kT_ready, i)
                        pe.wait_ge(xn_ready, i + 1)
                        for k in range(KB):
                            last = pe.transpose(tp[:, k, :], xn[:, k * P:(k + 1) * P], ident[:, :])
                        last.then_inc(turned, 1)
                        pe.wait_ge(hT_ready, i + 1)
                        pe.wait_ge(mm_loaded, 32)
                        for k in range(KB):
                            pe.matmul(g[0][:, 0:MW], hT[:, k, :], wbuf[:, 0, k, :], start=k == 0, stop=k == KB - 1)
                        for k in range(KB):
                            last = pe.matmul(g[0][:, MW:2 * MW], hT[:, k, :], wbuf[:, 1, k, :], start=k == 0, stop=k == KB - 1)
                        last.then_inc(gemm_done, 1)
                        pe.wait_ge(qkn_ready, i + 1)
                        for k in range(2):
                            last = pe.transpose(tp[:, k, :], xn[:, k * P:(k + 1) * P], ident[:, :])
                        last.then_inc(qk_turned, 1)
            end_block()


        def heads_of(ap, n):
            return ap.rearrange("p (h d) -> p h d", h=n)

        def prepare_sync(sp, e, c):
            R = c.rows
            if e is not None:
                sp.wait_ge(x2_copied, 1)
            sp.dma_start(x[:R, :], c.x_in).then_inc(x_loaded, 16)
            if c.sample:
                sp.wait_ge(copied, 1)
                sp.dma_start(v_all[:, 0:2, :], d_cache_a_v[0][0].rearrange("(b p) h d -> p b (h d)", p=P)).then_inc(cache_loaded, 16)
                sp.dma_start(mv[:, :, :], d_cache_m_v[0][0].rearrange("(b p) h d -> p b (h d)", p=P)).then_inc(cache_loaded, 16)
                for b in range(2):
                    sp.dma_start(logf[:, b, :], d_cache_a_logf[0][0][b * P:(b + 1) * P, :]).then_inc(cache_loaded, 16)
                    sp.dma_start(z[:, b * AW:(b + 1) * AW], d_cache_a_k[0][0][b * P:(b + 1) * P].rearrange("p h d -> p (h d)")).then_inc(cache_loaded, 16)
                    sp.dma_start(xn[:, b * MW:(b + 1) * MW], d_cache_m_k[0][0][b * P:(b + 1) * P].rearrange("p h d -> p (h d)")).then_inc(cache_loaded, 16)
                    with nc.allow_non_contiguous_dma("2 rows of history, channels to partitions"):
                        sp.dma_start(uT[:, b, 0:2], d_cache_b_conv[0][0][:, b * P:(b + 1) * P].rearrange("t c -> c t")).then_inc(cache_loaded, 16)
            w_in, w_out, w_pq = d_w_in[0], d_w_out[0], d_w_peer_q[0]
            cols = [w_in[:, i * CHUNK:(i + 1) * CHUNK] for i in range(6)] + [w_in[:, BCOL + i * CHUNK:BCOL + (i + 1) * CHUNK] for i in range(4)]
            cols += [w[:, i * CHUNK:(i + 1) * CHUNK] for w in (w_out, w_pq) for i in range(4)]
            for n in range(10):
                load_chunk(sp, n, cols[n])
            sp.wait_ge(z_ready, 3)
            sp.dma_start(c.v_out, z[:R, 2 * AW:3 * AW]).then_inc(stored, 16)
            sp.wait_ge(qkn_ready, 2)
            sp.dma_start(c.k_out, z[:R, AW:2 * AW]).then_inc(stored, 16)
            sp.wait_ge(logf_ready, 1)
            sp.dma_start(c.logf_out, lf[:R, 0, :]).then_inc(stored, 16)
            sp.wait_ge(u_ready, 1)
            for b in range(2):
                with nc.allow_non_contiguous_dma("2 rows of convolution state, channels on partitions"):
                    sp.dma_start(c.conv_out[:, b * P:(b + 1) * P].rearrange("t c -> c t"), uT[:, b, R:R + 2]).then_inc(stored, 16)
            for n in range(10, 18):
                load_chunk(sp, n, cols[n])
            sp.wait_ge(stored, 16 * 5)

        def prepare_tensor(pe, c):
            R, W = c.rows, c.blocks * P

            def rows_by_columns(n, out):
                pe.wait_ge(w_loaded[n % NW], 16 * (n // NW + 1))
                for k in range(KB):
                    last = pe.matmul(out, hT[:, k, :R], wbuf[:, n % NW, k, :], start=k == 0, stop=k == KB - 1)
                last.then_inc(gemm_done, 1)

            def columns_by_rows(n, bank, at):
                pe.wait_ge(w_loaded[n % NW], 16 * (n // NW + 1))
                for j in range(CHUNK // P):
                    for k in range(KB):
                        last = pe.matmul(bank[:, (at + j) * P:(at + j) * P + R], wbuf[:, n % NW, k, j * P:(j + 1) * P], hT[:, k, :R],
                                         start=k == 0, stop=k == KB - 1)
                last.then_inc(gemm_done, 1)

            def turn(dst, src, width, signal):
                for k in range(width // P):
                    last = pe.transpose(tp[:, dst + k, :R], src[:R, k * P:(k + 1) * P], ident[:R, :R])
                last.then_inc(signal, 1)

            yield "square"
            if c.sample:
                pe.wait_ge(cache_loaded, 16 * 10)
                for b in range(2):
                    if b:
                        pe.wait_ge(cache_copied, 1)
                    for k in range(4):
                        pe.transpose(tp[:, k, :], z[:, b * AW + k * P:b * AW + (k + 1) * P], ident[:, :])
                    for k in range(2):
                        last = pe.transpose(tp[:, 4 + k, :], xn[:, b * MW + k * P:b * MW + (k + 1) * P], ident[:, :])
                    last.then_inc(cache_turned, 1)
                for b in range(2):
                    if b:
                        pe.wait_ge(ft_used, 1)
                    pe.matmul(g[0][0:AH, 0:P], logf[:, b, :], upto[:, :], start=True, stop=True).then_inc(ft_done, 1)
                pe.wait_ge(cache_copied, 2)
                pe.wait_ge(ft_used, 2)
            yield "turn"
            pe.wait_ge(xn_ready, 1)
            turn(0, xn, D, turned)
            yield "w0"
            pe.wait_ge(hT_ready, 1)
            for k in range(KB):
                last = pe.matmul(tp[:R, 0, 0:AH], hT[:, k, :R], w_f[:, k, :], start=k == 0, stop=k == KB - 1)
            last.then_inc(fl_done, 1)
            for n in range(6):
                if n:
                    yield f"w{n}"
                if n == 4:
                    pe.wait_ge(z_ready, 1)
                rows_by_columns(n, g[n // 2 % 2][:R, n % 2 * CHUNK:(n % 2 + 1) * CHUNK])
            for n in (6, 7):
                yield f"w{n}"
                pe.wait_ge(z_ready, 2)
                columns_by_rows(n, g[1], n % 2 * 2)
            yield "w8"
            pe.wait_ge(z_ready, 3)
            columns_by_rows(8, g[0], 0)
            yield "w9"
            rows_by_columns(9, g[0][:R, CHUNK:BANK])
            yield "headsq"
            pe.wait_ge(logf_ready, 1)
            pe.wait_ge(bcT_ready, 1)
            pe.matmul(g[1][0:AH, 0:R], lf[:R, 0, :], upto[:R, :R], start=True, stop=True).then_inc(cum_done, 1)
            yield "turnqk"
            pe.wait_ge(f_ready, 1)
            pe.wait_ge(qkn_ready, 3)
            turn(0, z, 2 * AW, qk_turned)
            yield "turnqm"
            pe.wait_ge(qT_ready, 2)
            turn(0, z[:, 3 * AW:], MW, qm_turned)

            def scores(n):
                if n < AH:
                    for lo in range(0, W, BANK):
                        hi = min(lo + BANK, W)
                        pe.matmul(S[:R, lo:hi], qT[:, n, :R], kT[:, n // 2, lo:hi], start=True, stop=False)
                    pe.matmul(c.own_keys(S)[:R], ident[:R, :R], causal[:R, :R], start=False, stop=False)
                    for lo in range(0, W, BANK):
                        hi = min(lo + BANK, W)
                        last = pe.matmul(S[:R, lo:hi], headrow[:, n, :R], negF[:, lo:hi], start=False, stop=True)
                else:
                    last = pe.matmul(S[:R, 0:NMEM], qT[:, n, :R], mkT[:, (n - AH) // 2, :], start=True, stop=True)
                last.then_inc(s_done, 1)

            def blocks(n):
                return c.blocks if n < AH else NMEM // P

            yield "att0a"
            pe.wait_ge(kT_ready, 1)
            pe.wait_ge(qmT_ready, 2)
            pe.wait_ge(cum_used, 1)
            scores(0)
            for n in range(1, UNITS + 1):
                m = n - 1
                yield f"att{n}a"
                pe.wait_ge(exp_done, n)
                if m:
                    pe.wait_ge(pT_ready, m)
                turn(0, pr, blocks(m) * P, p_turned)
                if n < UNITS:
                    scores(n)
                yield f"att{n}c"
                pe.wait_ge(pT_ready, n)
                for b in range(blocks(m)):
                    if m < AH:
                        out, val = g[0][:R, m * HD:(m + 1) * HD], v_all[:, b, m * HD:(m + 1) * HD]
                    else:
                        out, val = g[1][:R, (m - AH) * HD:(m - AH + 1) * HD], mv[:, b, (m - AH) * HD:(m - AH + 1) * HD]
                    last = pe.matmul(out, pT[:, b, :R], val, start=b == 0, stop=b == blocks(m) - 1)
                last.then_inc(pv_done, 1)
            yield "turnmix"
            pe.wait_ge(mix_ready, 2)
            turn(0, xn, AW + MW, mix_turned)
            for n in range(10, 14):
                yield f"w{n}"
                if n == 10:
                    pe.wait_ge(mixT_ready, 2)
                    pe.wait_ge(conv_ready, 2)
                rows_by_columns(n, S[:R, (n - 10) * CHUNK:(n - 9) * CHUNK])
            yield "turn2"
            pe.wait_ge(xt_ready, 1)
            turn(0, xtn, D, xt_turned)
            for n in range(14, 18):
                yield f"w{n}"
                if n == 14:
                    pe.wait_ge(xtT_ready, 1)
                columns_by_rows(n, g[(n - 14) // 2], n % 2 * 2)
            for h in range(PH):
                yield "pqT" if h < 2 else f"top{h - 1}"
                pe.wait_ge(pqT_ready, h // 4 + 1)
                if h >= 2:
                    pe.wait_ge(ks_ready, h - 1)
                pe.matmul(S[:R, (h % 2) * BANK:(h % 2) * BANK + 2 * PKEYS], pT[:, h, :R], keys2[:, h, :], start=True, stop=True).then_inc(key_scores, 1)

        def prepare_scalar(sc_, c):
            R, W = c.rows, c.blocks * P

            def copy(dst, src, signal):
                sc_.activation(dst, src, ACT.Copy).then_inc(signal, 1)

            yield "square"
            sc_.wait_ge(x_loaded, 16)
            sc_.activation(pr[:R, :], x[:R, :], ACT.Square, accum_out=ss[:R, :]).then_inc(sq_done, 1)
            yield "root"
            sc_.wait_ge(rms_ready, 1)
            sc_.activation(ss[:R, :], ss[:R, :], ACT.Sqrt).then_inc(rms_ready, 1)
            for n, part in enumerate(("w2", "w4", "w6")):
                yield part
                sc_.wait_ge(gemm_done, 2 * n + 2)
                if c.sample:
                    sc_.wait_ge(cache_turned, 2)
                copy(z[:R, n * AW:(n + 1) * AW], g[n % 2][:R, :], z_ready)
            sc_.wait_ge(z_ready, 3)
            copy(c.own_values, z[:R, 2 * AW:3 * AW], kT_ready)
            sc_.wait_ge(f_ready, 1)
            sc_.activation(lf[:R, 2, :], lf[:R, 1, :], ACT.Exp).then_inc(f_exp, 1)
            sc_.wait_ge(f_exp, 1)
            sc_.activation(lf[:R, 3, :], lf[:R, 2, :], ACT.Ln, bias=1.0).then_inc(f_ln, 1)
            yield "w8"
            sc_.wait_ge(gemm_done, 8)
            copy(bcT[:, :, :R], g[1][:, :].rearrange("p (j q) -> p j q", j=4)[:, :, :R], bcT_ready)
            yield "qm"
            sc_.wait_ge(gemm_done, 10)
            copy(z[:R, 3 * AW:3 * AW + MW], g[0][:R, MW:2 * MW], z_ready)
            yield "headroot"
            sc_.wait_ge(qk_squares, 1)
            sc_.activation(hss[:R, :], hss[:R, :], ACT.Sqrt).then_inc(qk_rms, 1)
            for n in range(UNITS + 1):
                yield f"att{n}b"
                if n:
                    m = n - 1
                    nb = c.blocks if m < AH else NMEM // P
                    sc_.wait_ge(p_turned, n)
                    if m:
                        sc_.wait_ge(pv_done, m)
                    copy(pT[:, 0:nb, :R], tp[:, 0:nb, :R], pT_ready)
                if n < UNITS:
                    yield f"att{n}c"
                    w = W if n < AH else NMEM
                    sc_.wait_ge(nmax_ready, n + 1)
                    sc_.activation(pr[:R, 0:w], S[:R, 0:w], ACT.Exp, bias=nmax[:R, n:n + 1], accum_out=rsum[:R, n:n + 1]).then_inc(exp_done, 1)
            yield "mixT"
            sc_.wait_ge(mix_turned, 1)
            copy(mixT[:, 0:4, :R], tp[:, 0:4, :R], mixT_ready)
            copy(mixT[:, 6:8, :R], tp[:, 4:6, :R], mixT_ready)
            yield "square2"
            sc_.wait_ge(x2_ready, 1)
            sc_.activation(pr[:R, :], x2n[:R, :], ACT.Square, accum_out=ss[:R, :]).then_inc(sq2_done, 1)
            yield "root2"
            sc_.wait_ge(rms2_ready, 1)
            sc_.activation(ss[:R, :], ss[:R, :], ACT.Sqrt).then_inc(rms2_ready, 1)
            yield "xtT"
            sc_.wait_ge(xt_turned, 1)
            copy(hT[:, :, :R], tp[:, :, :R], xtT_ready)
            for i, part in enumerate(("w16", "pqT")):
                yield part
                sc_.wait_ge(gemm_done, 16 + 2 * i)
                copy(pT[:, 4 * i:4 * i + 4, :R], g[i][:, :].rearrange("p (j q) -> p j q", j=4)[:, :, :R], pqT_ready)
            for h in range(PH):
                if h:
                    yield f"top{h}"
                sc_.wait_ge(key_scores, h + 1)
                if h >= 2:
                    sc_.wait_ge(picked, h - 1)
                copy(ks[:R, h % 2, :], S[:R, (h % 2) * BANK:(h % 2) * BANK + 2 * PKEYS], ks_ready)
            yield "gate1"
            sc_.wait_ge(diff_ready, 1)
            sc_.activation(ex[:R, :, :], ex[:R, :, :], ACT.Exp).then_inc(ex_ready, 1)

        def prepare_vector(v, c, chain):
            R, W = c.rows, c.blocks * P
            do = chain.do
            yield "square"
            if c.sample:
                for b in range(2):
                    v.wait_ge(cache_turned, b + 1)
                    do(v.tensor_copy(kT[:, :, b * P:(b + 1) * P], tp[:, 0:4, :]))
                    v.tensor_copy(mkT[:, :, b * P:(b + 1) * P], tp[:, 4:6, :]).then_inc(cache_copied, 1)
                do(v.memset(negF[0:AH, PAST:PAST + P], NEG))
                do(v.memset(ncarry[:, :], 0.0))
                for b in range(2):
                    v.wait_ge(ft_done, b + 1)
                    do(v.tensor_scalar(negF[0:AH, b * P:(b + 1) * P], g[0][0:AH, 0:P], -1.0, ncarry[:, 0:1], ALU.mult, ALU.add))
                    v.tensor_scalar(ncarry[:, :], g[0][0:AH, P - 1:P], -1.0, ncarry[:, 0:1], ALU.mult, ALU.add).then_inc(ft_used, 1)
                    v.wait_ge(ft_used, b + 1)
                v.wait_ge(cache_loaded, 16 * 10)
            yield "rms"
            v.wait_ge(sq_done, 1)
            v.tensor_scalar(ss[:R, :], ss[:R, :], 1.0 / D, EPS, ALU.mult, ALU.add).then_inc(rms_ready, 1)
            yield "scale"
            v.wait_ge(rms_ready, 2)
            do(v.reciprocal(rstd[:R, :], ss[:R, :]))
            v.tensor_scalar(xn[:R, :], x[:R, :], rstd[:R, 0:1], None, ALU.mult).then_inc(xn_ready, 1)
            yield "hT"
            v.wait_ge(turned, 1)
            v.tensor_tensor(hT[:, :, :R], tp[:, :, :R], g_attn[:, :].unsqueeze(2).to_broadcast([P, KB, R]), ALU.mult).then_inc(hT_ready, 1)
            yield "w1"
            v.wait_ge(fl_done, 1)
            do(v.tensor_tensor(lf[:R, 0, :], tp[:R, 0, 0:AH], bias_f[:R, :], ALU.add))
            do(v.tensor_scalar(lf[:R, 1, :], lf[:R, 0, :], -1.0, None, ALU.mult))
            v.tensor_tensor(lf[:R, 1, :], lf[:R, 1, :], lf[:R, 0, :], ALU.min).then_inc(f_ready, 1)
            yield "w7"
            v.wait_ge(f_ln, 1)
            do(v.tensor_scalar(lf[:R, 0, :], lf[:R, 0, :], 0.0, None, ALU.min))
            v.tensor_tensor(lf[:R, 0, :], lf[:R, 0, :], lf[:R, 3, :], ALU.subtract).then_inc(logf_ready, 1)
            yield "conv"
            v.wait_ge(gemm_done, 10)
            v.wait_ge(bcT_ready, 1)
            v.wait_ge(z_ready, 4)
            v.tensor_tensor(uT[:, :, 2:2 + R], bcT[:, 2:4, :R], g[0][:, 0:2 * P].rearrange("p (j q) -> p j q", j=2)[:, :, :R], ALU.mult).then_inc(u_ready, 1)
            v.wait_ge(u_ready, 1)
            for b in range(2):
                do(v.tensor_scalar(yT[:, b, :R], uT[:, b, 2:2 + R], conv_w[:, b, 2:3], conv_b[:, b:b + 1], ALU.mult, ALU.add))
                for j in range(2):
                    do(v.scalar_tensor_tensor(yT[:, b, :R], uT[:, b, j:j + R], conv_w[:, b, j:j + 1], yT[:, b, :R], ALU.mult, ALU.add))
                v.tensor_tensor(mixT[:, 4 + b, :R], yT[:, b, :R], bcT[:, b, :R], ALU.mult).then_inc(conv_ready, 1)
            yield "headsq"
            v.wait_ge(z_ready, 4)
            do(v.tensor_tensor(pr[:R, :], z[:R, 0:2 * AW], z[:R, 0:2 * AW], ALU.mult))
            do(v.tensor_reduce(hss[:R, 0:16], heads_of(pr[:R, :], 16), AX, ALU.add))
            do(v.tensor_tensor(pr[:R, 0:MW], z[:R, 3 * AW:3 * AW + MW], z[:R, 3 * AW:3 * AW + MW], ALU.mult))
            do(v.tensor_reduce(hss[:R, 16:20], heads_of(pr[:R, 0:MW], MH), AX, ALU.add))
            v.tensor_scalar(hss[:R, :], hss[:R, :], 1.0 / HD, EPS, ALU.mult, ALU.add).then_inc(qk_squares, 1)
            yield "headnorm"
            v.wait_ge(qk_rms, 1)
            do(v.reciprocal(hrs[:R, :], hss[:R, :]))
            for lo, h0, nh, gain in ((0, 0, AH, g_q), (AW, AH, AH, g_k), (3 * AW, 2 * AH, MH, g_qm)):
                zz = heads_of(z[:R, lo:lo + nh * HD], nh)
                do(v.tensor_tensor(zz, zz, hrs[:R, h0:h0 + nh].unsqueeze(2).to_broadcast([R, nh, HD]), ALU.mult))
                v.tensor_tensor(zz, zz, gain[:R, :].unsqueeze(1).to_broadcast([R, nh, HD]), ALU.mult).then_inc(qkn_ready, 1)
            v.wait_ge(cum_done, 1)
            do(v.tensor_scalar(c.own_negF, g[1][0:AH, 0:R], -1.0, ncarry[:, 0:1], ALU.mult, ALU.add))
            v.tensor_scalar(ncarry[:, :], g[1][0:AH, R - 1:R], -1.0, ncarry[:, 0:1], ALU.mult, ALU.add).then_inc(cum_used, 1)
            yield "qT"
            v.wait_ge(qk_turned, 1)
            v.tensor_copy(qT[0:HD, 0:AH:2, :R], tp[0:HD, 0:4, :R]).then_inc(qT_ready, 1)
            v.tensor_copy(qT[HD:P, 1:AH:2, :R], tp[HD:P, 0:4, :R]).then_inc(qT_ready, 1)
            do(v.tensor_copy(c.own_keysT, tp[:, 4:8, :R]))
            yield "qmT"
            v.wait_ge(qm_turned, 1)
            v.tensor_copy(qT[0:HD, AH:UNITS:2, :R], tp[0:HD, 0:2, :R]).then_inc(qmT_ready, 1)
            v.tensor_copy(qT[HD:P, AH + 1:UNITS:2, :R], tp[HD:P, 0:2, :R]).then_inc(qmT_ready, 1)
            for n in range(UNITS):
                yield f"att{n}b"
                v.wait_ge(s_done, n + 1)
                v.tensor_reduce(nmax[:R, n:n + 1], S[:R, 0:W if n < AH else NMEM], AX, ALU.max, negate=True).then_inc(nmax_ready, 1)
            yield "mix"
            v.wait_ge(exp_done, UNITS)
            do(v.reciprocal(rinv[:R, :], rsum[:R, :]))
            v.wait_ge(pv_done, UNITS)
            v.tensor_tensor(heads_of(xn[:R, 0:AW], AH), heads_of(g[0][:R, :], AH), rinv[:R, 0:AH].unsqueeze(2).to_broadcast([R, AH, HD]), ALU.mult).then_inc(mix_ready, 1)
            v.tensor_tensor(heads_of(xn[:R, AW:AW + MW], MH), heads_of(g[1][:R, 0:MW], MH), rinv[:R, AH:UNITS].unsqueeze(2).to_broadcast([R, MH, HD]), ALU.mult).then_inc(mix_ready, 1)
            v.wait_ge(conv_ready, 2)
            v.wait_ge(stored, 16 * 5)
            do(v.tensor_copy(uT[:, :, 0:2], uT[:, :, R:R + 2]))
            yield "residual"
            v.wait_ge(gemm_done, 14)
            v.tensor_tensor(x2n[:R, :], S[:R, :], x[:R, :], ALU.add).then_inc(x2_ready, 1)
            yield "rms2"
            v.wait_ge(sq2_done, 1)
            v.tensor_scalar(ss[:R, :], ss[:R, :], 1.0 / D, EPS, ALU.mult, ALU.add).then_inc(rms2_ready, 1)
            yield "scale2"
            v.wait_ge(rms2_ready, 2)
            do(v.reciprocal(rstd[:R, :], ss[:R, :]))
            v.scalar_tensor_tensor(xtn[:R, :], x2n[:R, :], rstd[:R, 0:1], g_ffn[:R, :], ALU.mult, ALU.mult).then_inc(xt_ready, 1)
            add, settle = chain.add, chain.settle
            for h in range(PH + 1):
                yield f"top{h}"
                best, look = h < PH, h >= 1
                if best:
                    v.wait_ge(ks_ready, h + 1)
                    kq = [ks[:R, h % 2, q * PKEYS:(q + 1) * PKEYS] for q in range(2)]
                    for q in range(2):
                        add(v.max(pick[:R, q, 0:8], kq[q]))
                if look:
                    add(v.tensor_scalar(cij[:R, 0, :], ci[:R, :], 4, None, ALU.logical_shift_right))
                    add(v.tensor_scalar(cij[:R, 1, :], ci[:R, :], TOPK - 1, None, ALU.bitwise_and))
                    add(v.tensor_copy(pickf[:R, :, :], picki[:R, :, :]))
                settle()
                if best:
                    for q in range(2):
                        add(v.max_index(picki[:R, q, 0:8], pick[:R, q, 0:8], kq[q]))
                        ins = v.match_replace(left[:R, q, :], pick[:R, q, 0:8], kq[q], GONE)
                        if q == 0:
                            add(ins)
                        else:
                            ins.then_inc(picked, 1)
                if look:
                    add(v.tensor_copy(cijf[:R, :, :], cij[:R, :, :]))
                settle()
                if best:
                    v.wait_ge(picked, h + 1)
                    for q in range(2):
                        add(v.max(pick[:R, q, 8:16], left[:R, q, :]))
                if look:
                    add(v.tensor_tensor(onehot[:R], iota16[:R, :].unsqueeze(1).unsqueeze(1).to_broadcast([R, 2, TOPK, TOPK]),
                                        cijf[:R, :, :].unsqueeze(3).to_broadcast([R, 2, TOPK, TOPK]), ALU.is_equal))
                settle()
                if best:
                    for q in range(2):
                        add(v.max_index(picki[:R, q, 8:16], pick[:R, q, 8:16], left[:R, q, :]))
                    add(v.tensor_tensor(cand[:R, :, :], pick[:R, 0, :].unsqueeze(2).to_broadcast([R, TOPK, TOPK]),
                                        pick[:R, 1, :].unsqueeze(1).to_broadcast([R, TOPK, TOPK]), ALU.add))
                if look:
                    add(v.tensor_tensor(onehot[:R], onehot[:R], pickf[:R, :, :].unsqueeze(2).to_broadcast([R, 2, TOPK, TOPK]), ALU.mult))
                settle()
                cands = cand[:R, :, :].rearrange("p i j -> p (i j)")
                if best:
                    add(v.max(sc[:R, h, 0:8], cands))
                if look:
                    add(v.tensor_reduce(e12[:R, :, :], onehot[:R], AX, ALU.add))
                settle()
                if best:
                    add(v.max_index(ci[:R, 0:8], sc[:R, h, 0:8], cands))
                    add(v.match_replace(candleft[:R, :], sc[:R, h, 0:8], cands, GONE))
                if look:
                    ins = v.scalar_tensor_tensor(idxn[:R, h - 1, :], e12[:R, 0, :], float(PKEYS), e12[:R, 1, :], ALU.mult, ALU.add)
                    if h == 1:
                        ins.then_inc(first_picked, 1)
                        v.wait_ge(first_picked, 1)
                    else:
                        add(ins)
                settle()
                if best:
                    add(v.max(sc[:R, h, 8:16], candleft[:R, :]))
                    settle()
                    add(v.max_index(ci[:R, 8:16], sc[:R, h, 8:16], candleft[:R, :]))
                    settle()
            yield "gate0"
            v.tensor_tensor(ex[:R, :, :], sc[:R, :, :], sc[:R, :, 0:1].to_broadcast([R, PH, TOPK]), ALU.subtract).then_inc(diff_ready, 1)
            yield "gate2"
            v.wait_ge(ex_ready, 1)
            do(v.tensor_reduce(esum[:R, :], ex[:R, :, :], AX, ALU.add))
            do(v.reciprocal(esum[:R, :], esum[:R, :]))
            do(v.tensor_tensor(gaten[:R, :, :], ex[:R, :, :], esum[:R, :].unsqueeze(2).to_broadcast([R, PH, TOPK]), ALU.mult))


        def wait_v_used(eng, e, m):
            if e.on_vector(m):
                eng.wait_ge(v_added, e.vector_slots(m))
            else:
                eng.wait_ge(v_used, e.tensor_slots(m))

        def gather_u(pool, R, n, index):
            pool.indirect_dma_start(urow[:R, n % NU, :], None, d_peer_u[0], bass.IndirectOffsetOnAxis(ap=index, axis=0)).then_inc(u_landed[n % NU], 16)

        def gathers(pool, e, c):
            if e is not None:
                if e.groups == 1:
                    for n in range(AHEAD, NU):
                        gather_u(pool, P, n, idxn[:, 0, n:n + 1])
                    pool.wait_ge(copied, 2)
                    asked = NU
                else:
                    pool.wait_ge(idx_spread, 16 * e.groups)
                    asked = 0
                for n in range(asked, e.steps):
                    if n < e.slots:
                        if n >= NU:
                            pool.wait_ge(dots, n - NU + 1)
                        gather_u(pool, P, n, idx[:, n:n + 1])
                    m = n - VLAG
                    if m >= 0:
                        if m >= NV:
                            wait_v_used(pool, e, m - NV)
                        pool.indirect_dma_start(vrow[:, m % NV, :], None, d_peer_v[0], bass.IndirectOffsetOnAxis(ap=idx[:, m:m + 1], axis=0)).then_inc(v_landed[m % NV], 16)
            ahead = AHEAD if c is not None and not c.sample else 0
            if ahead:
                pool.wait_ge(first_picked, 1)
                if e is not None:
                    pool.wait_ge(dots, e.slots)
                for n in range(ahead):
                    gather_u(pool, P, n, idxn[:, 0, n:n + 1])
            for i in range(NU):
                turns = (e.landings(e.slots - 1 - (e.slots - 1 - i) % NU) if e is not None else 0) + (i < ahead)
                if turns:
                    pool.wait_ge(u_landed[i], 16 * turns)
            if e is not None:
                for i in range(NV):
                    pool.wait_ge(v_landed[i], 16 * ((e.slots - 1 - i) // NV + 1))
            pool.dma_reset()

        def spread_sync(sp, e):
            indices, gates = idxn.rearrange("p h k -> p (h k)"), gaten.rearrange("p h k -> p (h k)")
            gate_flat = gate.rearrange("p h k -> p (h k)")
            for dst, src, signal in ((idx, indices, idx_spread), (xt, None, xt_spread), (gate_flat, gates, gate_spread)):
                for i in range(e.groups):
                    rows = slice(i * e.tokens, (i + 1) * e.tokens)
                    if src is None:
                        sp.dma_start(dst[rows, :], xtn[:e.tokens, :]).then_inc(signal, 16)
                    else:
                        sp.dma_start(dst[rows, 0:e.slots], src[:e.tokens, i * e.slots:(i + 1) * e.slots]).then_inc(signal, 16)

        def experts_vector(v, e):
            if e.groups == 1:
                v.tensor_copy(xt[:, :], xtn[:, :]).then_inc(copied, 1)
                v.tensor_copy(idx[:, :], idxn[:, :, :].rearrange("p h k -> p (h k)")).then_inc(copied, 1)
                v.tensor_copy(gate[:, :, :], gaten[:, :, :]).then_inc(copied, 1)
                v.wait_ge(copied, 3)
            else:
                v.memset(acc2[:, :], 0.0).then_inc(acc2_zeroed, 1)
                v.wait_ge(xt_spread, 16 * e.groups)
                v.wait_ge(gate_spread, 16 * e.groups)
            for n in range(e.steps):
                yield n
                if n < e.slots:
                    if e.landings(n):
                        v.wait_ge(u_landed[n % NU], 16 * e.landings(n))
                    u = urow[:, n % NU, :]
                    v.tensor_tensor_reduce(u, u, xt[:, :], 1.0, 0.0, ALU.mult, ALU.add, act[:, n // TOPK, n % TOPK:n % TOPK + 1]).then_inc(dots, 1)
                if n % TOPK == 4 and TOPK <= n < e.slots + TOPK:
                    h = n // TOPK - 1
                    v.wait_ge(gelu_done, h + 1)
                    v.tensor_tensor(wgt[:, h * TOPK:(h + 1) * TOPK], gel[:, h, :], gate[:, h, :], ALU.mult).then_inc(wgt_ready, 1)
                m = n - VLAG
                if m >= 0 and e.on_vector(m):
                    v.wait_ge(v_landed[m % NV], 16 * (m // NV + 1))
                    v.wait_ge(wgt_ready, m // TOPK + 1)
                    if e.vector_slots(m) == 1:
                        v.wait_ge(x2_copied, 1)
                    else:
                        v.wait_ge(v_added, e.vector_slots(m) - 1)
                    v.scalar_tensor_tensor(acc2[:, :], vrow[:, m % NV, :], wgt[:, m:m + 1], acc2[:, :], ALU.mult, ALU.add).then_inc(v_added, 1)
            last = e.slots - 1
            if e.groups == 1:
                v.wait_ge(v_added, e.vector_slots(last))
                v.wait_ge(v_used, e.tensor_slots(last))
                v.tensor_tensor(acc2[:, :], acc2[:, :], acc[:, :], ALU.add).then_inc(y_ready, 1)
            else:
                v.wait_ge(v_used, e.tensor_slots(last) + 1)
                v.tensor_copy(acc2[:e.tokens, :], acc[:e.tokens, :]).then_inc(y_ready, 1)

        def experts_scalar(sc_, e):
            if e.groups > 1:
                sc_.wait_ge(acc2_zeroed, 1)
            sc_.activation(acc2[:e.tokens, :], x2n[:e.tokens, :], ACT.Copy).then_inc(x2_copied, 1)
            places = ident if e.groups == 1 else fold
            for n in range(e.steps):
                yield n
                if n % TOPK == 2 and TOPK <= n < e.slots + TOPK:
                    h = n // TOPK - 1
                    sc_.wait_ge(dots, (h + 1) * TOPK)
                    sc_.activation(gel[:, h, :], act[:, h, :], ACT.Gelu).then_inc(gelu_done, 1)
                m = n - VLAG + 2
                if 0 <= m < e.slots and not e.on_vector(m):
                    j = e.tensor_slots(m) - 1
                    sc_.wait_ge(wgt_ready, m // TOPK + 1)
                    if j >= ND:
                        sc_.wait_ge(v_used, j - ND + 1)
                    sc_.activation(diag[:, j % ND, :e.tokens], places[:, :e.tokens], ACT.Copy, scale=wgt[:, m:m + 1]).then_inc(diag_ready, 1)

        def experts_tensor(pe, e):
            last = e.tensor_slots(e.slots - 1) - 1
            for n in range(e.steps):
                yield n
                m = n - VLAG
                if m >= 0 and not e.on_vector(m):
                    j = e.tensor_slots(m) - 1
                    pe.wait_ge(diag_ready, j + 1)
                    pe.wait_ge(v_landed[m % NV], 16 * (m // NV + 1))
                    for i in range(2):
                        ins = pe.matmul(acc[:e.tokens, i * BANK:(i + 1) * BANK], diag[:, j % ND, :e.tokens], vrow[:, m % NV, i * BANK:(i + 1) * BANK],
                                        start=j == 0, stop=j == last and e.groups == 1)
                    ins.then_inc(v_used, 1)
            if e.groups > 1:
                pe.wait_ge(v_added, e.vector_slots(e.slots - 1))
                for i in range(2):
                    ins = pe.matmul(acc[:e.tokens, i * BANK:(i + 1) * BANK], fold[:, :], acc2[:, i * BANK:(i + 1) * BANK], start=False, stop=True)
                ins.then_inc(v_used, 1)

        def block_of(e, c):
            def both(experts, prepare):
                beside(experts if experts is not None else [], [prepare, None] if prepare is not None else None)

            with nc.Block() as block:
                @block.sync
                def _(sp):
                    if e is not None and e.groups > 1:
                        spread_sync(sp, e)
                    if c is not None:
                        prepare_sync(sp, e, c)
                    if e is not None:
                        sp.wait_ge(y_ready, 1)
                        sp.dma_start(e.y_out, acc2[:e.tokens, :]).then_inc(y_stored, 16)
                        sp.wait_ge(y_stored, 16)

                @block.gpsimd
                def _(pool):
                    gathers(pool, e, c)

                @block.vector
                def _(v):
                    both(experts_vector(v, e) if e is not None else None, prepare_vector(v, c, Chain(v, dve_chain)) if c is not None else None)

                @block.scalar
                def _(sc_):
                    both(experts_scalar(sc_, e) if e is not None else None, prepare_scalar(sc_, c) if c is not None else None)

                @block.tensor
                def _(pe):
                    both(experts_tensor(pe, e) if e is not None else None, prepare_tensor(pe, c) if c is not None else None)
            end_block()

        def prompt_tile(t, blocks):
            rows = bass.ds(t * P, P)
            return NextTile(
                rows=P, blocks=blocks, sample=False, x_in=d_x_prompt[0][rows, :],
                own_keys=lambda m: m[:, rows], own_keysT=kT[:, :, rows], own_negF=negF[0:AH, rows],
                own_values=v_all[:, bass.ds(t, 1), :].rearrange("p a n -> p (a n)"),
                k_out=d_a_k[0][0][rows].rearrange("n h d -> n (h d)"), v_out=d_a_v[0][0][rows].rearrange("n h d -> n (h d)"),
                logf_out=d_a_logf[0][0][rows, :], conv_out=d_b_conv[0][0])

        sample_tile = NextTile(
            rows=NEW, blocks=3, sample=True, x_in=d_x_sample[0],
            own_keys=lambda m: m[:, PAST:PAST + NEW], own_keysT=kT[:, :, PAST:PAST + NEW], own_negF=negF[0:AH, PAST:PAST + NEW],
            own_values=v_all[0:NEW, 2, :],
            k_out=d_a_k_s[0][0].rearrange("n h d -> n (h d)"), v_out=d_a_v_s[0][0].rearrange("n h d -> n (h d)"),
            logf_out=d_a_logf_s[0][0], conv_out=d_b_conv_s[0][0])

        def prompt_experts(t):
            return Tile(P, d_y_prompt[0][bass.ds(t * P, P), :])

        setup()
        block_of(None, prompt_tile(0, 1))
        for first, last, blocks in ((0, TILES // 2 - 1, TILES // 2), (TILES // 2 - 1, TILES - 1, TILES)):
            with nc.Fori(first, last) as t:
                block_of(prompt_experts(t), prompt_tile(t + 1, blocks))
        block_of(prompt_experts(TILES - 1), sample_tile)
        block_of(Tile(NEW, d_y_sample[0], alone=True), None)


_INS = ['x_prompt', 'x_sample', 'cache_a_k', 'cache_a_v', 'cache_a_logf', 'cache_b_conv', 'cache_m_k', 'cache_m_v',
        'mem_prompt', 'g_attn', 'w_in', 'b_f', 'g_q_a', 'g_k_a', 'conv_w', 'conv_b', 'g_mem', 'w_mem_k', 'w_mem_v',
        'g_k_m', 'g_q_m', 'w_out', 'g_ffn', 'w_peer_q', 'peer_keys', 'peer_u', 'peer_v']
_OUTS = [('y_prompt', (1, 1024, 1024)), ('y_sample', (1, 32, 1024)), ('a_k', (1, 1, 1024, 8, 64)), ('a_v', (1, 1, 1024, 8, 64)),
         ('a_logf', (1, 1, 1024, 8)), ('b_conv', (1, 1, 2, 256)), ('m_k', (1, 1, 256, 4, 64)), ('m_v', (1, 1, 256, 4, 64)),
         ('a_k_s', (1, 1, 32, 8, 64)), ('a_v_s', (1, 1, 32, 8, 64)), ('a_logf_s', (1, 1, 32, 8)), ('b_conv_s', (1, 1, 2, 256))]


def kernel(**inputs):
    import numpy as _np
    import concourse.bacc as _bacc
    from concourse import mybir as _mybir
    from concourse.bass_utils import run_bass_kernel_spmd as _run

    nc = _bacc.Bacc("TRN2", target_bir_lowering=False, num_devices=1)
    arrays, args = {}, []
    for name in _INS:
        v = _np.ascontiguousarray(inputs[name])
        arrays[f"in_{name}_dram"] = v
        args.append(nc.dram_tensor(f"in_{name}_dram", v.shape, _mybir.dt.from_np(v.dtype), kind="ExternalInput").ap())
    for name, shape in _OUTS:
        args.append(nc.dram_tensor(f"out_{name}_dram", shape, F32, kind="ExternalOutput").ap())
    build(nc, *args)
    r = _run(nc, [arrays], core_ids=[0])
    return tuple(r.results[0][f"out_{name}_dram"] for name, _ in _OUTS)
```

```python
from contextlib import ExitStack

import concourse.bass as bass
from concourse import mybir

F32 = mybir.dt.float32
U32 = mybir.dt.uint32
ALU = mybir.AluOpType
ACT = mybir.ActivationFunctionType
AX = mybir.AxisListType.X

P = 128
D = 1024
KB = D // P
SEQ, NEW, PAST, NMEM = 1024, 32, 256, 256
TILES = SEQ // P
AH, MH, HD = 8, 4, 64
AW, BW, MW = AH * HD, 256, MH * HD
FCOL = 3 * AW
BCOL = FCOL + AH
BANK = 512
CHUNK = 256
PH, PKEYS, TOPK = 8, 128, 16
SLOTS = PH * TOPK
NEXP = PKEYS * PKEYS
EPS = 1e-6
NEG = -1e30
GONE = -3e38
UNITS = AH + MH
NU, NV, ND, NW = 6, 6, 4, 4
VLAG = 24
AHEAD = 4


class Tile:

    def __init__(self, tokens, y_out, beside=None):
        self.tokens, self.y_out, self.beside = tokens, y_out, beside
        self.groups = P // tokens
        self.slots = SLOTS // self.groups
        self.steps = self.slots + VLAG
        self.ahead = AHEAD if self.groups == 1 else 0

    def on_vector(self, m):
        if self.beside is not None:
            at, step = AT[self.beside], m + VLAG
            if at["top0"] <= step < SLOTS:
                return False
            if self.beside == FIRST and at["w0"] <= step < at["headsq"]:
                return True
        return m % 2 == 1

    def vector_slots(self, m):
        return sum(self.on_vector(i) for i in range(m + 1))

    def tensor_slots(self, m):
        return m + 1 - self.vector_slots(m)

    def landings(self, n):
        return n // NU + (n % NU >= self.ahead)


class Chain:

    def __init__(self, eng, sem):
        self.eng, self.sem, self.n = eng, sem, 0

    def add(self, ins):
        self.n += 1
        ins.then_inc(self.sem, 1)

    def settle(self):
        self.eng.wait_ge(self.sem, self.n)

    def do(self, ins):
        self.add(ins)
        self.settle()


ALONE, FIRST, SECOND = "alone", "first", "second"


def parts_of(kind):
    if kind == SECOND:
        parts = [("square", 5), ("cache", 3), ("w1", 1), ("w6", 1), ("w7", 1)]
    else:
        parts = [("square", 1), ("rms", 1), ("root", 1), ("scale", 1), ("turn", 1), ("hT", 1)]
        if kind == FIRST:
            parts += [("mate_square", 1), ("mate_rms", 1), ("mate_root", 1), ("mate_scale", 1), ("mate_turn", 1), ("mate_hT", 1)]
        for n in range(10):
            parts.append((f"w{n}", 2))
            if kind == FIRST:
                parts.append((f"mate{n}", 2))
    parts += [("qm", .5), ("conv", 1), ("headsq", 2), ("headroot", .5), ("headnorm", 3), ("turnqk", 1), ("qT", 1), ("turnqm", .5), ("qmT", .5)]
    parts += [(f"att{n}{x}", 1 if n <= AH else .7) for n in range(UNITS + 1) for x in "abc"]
    parts += [("mix", 1), ("turnmix", 1), ("mixT", .5)] + [(f"w{n}", 2) for n in range(10, 14)]
    parts += [("residual", .5), ("square2", .5), ("rms2", .5), ("root2", .5), ("scale2", 1), ("turn2", 1), ("xtT", .5)]
    parts += [(f"w{n}", 2) for n in range(14, 18)] + [("pqT", .5)]
    parts += [(f"top{h}", 6 if kind == FIRST else 5.2) for h in range(PH)] + [(f"top{PH}", 1)] + [("gate0", .5), ("gate1", .5), ("gate2", 0)]
    return parts


def part_steps(parts):
    at, steps, total = 0, {}, sum(w for _, w in parts)
    for part, w in parts:
        time = at / total * (2 * SLOTS - VLAG)
        steps[part] = int(time if time < VLAG else VLAG + (time - VLAG) / 2)
        at += w
    return steps


AT = {kind: part_steps(parts_of(kind)) for kind in (ALONE, FIRST, SECOND)}


def beside(experts, prepare, at):
    for n in experts:
        while prepare is not None:
            if prepare[1] is None or at[prepare[1]] <= n:
                prepare[1] = next(prepare[0], False)
                if prepare[1] is False:
                    prepare = None
            else:
                break
    if prepare is not None:
        for _ in prepare[0]:
            pass


class NextTile:

    def __init__(self, kind, mate, rows, blocks, sample, x_in, own_keys, own_keysT, own_negF, own_values, k_out, v_out, logf_out, conv_out):
        self.kind, self.mate = kind, mate
        self.rows, self.blocks, self.sample, self.x_in = rows, blocks, sample, x_in
        self.own_keys, self.own_keysT, self.own_negF, self.own_values = own_keys, own_keysT, own_negF, own_values
        self.k_out, self.v_out, self.logf_out, self.conv_out = k_out, v_out, logf_out, conv_out
        self.chunk0 = 10 if kind == SECOND else 0


class Mate:

    def __init__(self, rows, x_in):
        self.rows, self.x_in = rows, x_in


def build(nc, d_x_prompt, d_x_sample, d_cache_a_k, d_cache_a_v, d_cache_a_logf, d_cache_b_conv, d_cache_m_k, d_cache_m_v, d_mem_prompt, d_g_attn, d_w_in, d_b_f, d_g_q_a, d_g_k_a, d_conv_w, d_conv_b, d_g_mem, d_w_mem_k, d_w_mem_v, d_g_k_m, d_g_q_m, d_w_out, d_g_ffn, d_w_peer_q, d_peer_keys, d_peer_u, d_peer_v,
          d_y_prompt, d_y_sample, d_a_k, d_a_v, d_a_logf, d_b_conv, d_m_k, d_m_v, d_a_k_s, d_a_v_s, d_a_logf_s, d_b_conv_s):
    with ExitStack() as ctx:
        def sb(name, shape, dt=F32):
            return ctx.enter_context(nc.sbuf_tensor(name, shape, dt))

        ident = sb("ident", [P, P])
        upto = sb("upto", [P, P])
        causal = sb("causal", [P, P])
        headrow = sb("headrow", [P, AH, P])
        fold = sb("fold", [P, NEW])
        iota16 = sb("iota16", [P, TOPK])
        g_attn = sb("g_attn", [P, KB])
        g_mem = sb("g_mem", [P, KB])
        g_ffn = sb("g_ffn", [P, D])
        g_q = sb("g_q", [P, HD])
        g_k = sb("g_k", [P, HD])
        g_qm = sb("g_qm", [P, HD])
        g_km = sb("g_km", [P, HD])
        bias_f = sb("bias_f", [P, AH])
        conv_w = sb("conv_w", [P, 2, 3])
        conv_b = sb("conv_b", [P, 2])
        w_f = sb("w_f", [P, KB, AH])
        keys2 = sb("keys2", [P, PH, 2 * PKEYS])
        kT = sb("kT", [P, AH // 2, SEQ])
        v_all = sb("v_all", [P, TILES, AW])
        negF = sb("negF", [P, SEQ])
        ncarry = sb("ncarry", [AH, 1])
        mkT = sb("mkT", [P, MH // 2, NMEM])
        mv = sb("mv", [P, NMEM // P, MW])
        wbuf = sb("wbuf", [P, NW, KB, CHUNK])
        x = sb("x", [P, D])
        xn = sb("xn", [P, D])
        hT = sb("hT", [P, KB, P])
        mixT = hT
        z = sb("z", [P, 3 * AW + MW])
        qT = sb("qT", [P, UNITS, P])
        pr = sb("pr", [P, SEQ])
        pT = sb("pT", [P, TILES, P])
        uT = sb("uT", [P, 2, 2 + P])
        bcT = sb("bcT", [P, 4, P])
        yT = sb("yT", [P, 2, P])
        mate_z = sb("mate_z", [P, 3 * AW + MW])
        mate_bcT = sb("mate_bcT", [P, 6, P])
        mate_f = sb("mate_f", [P, AH])
        ss = sb("ss", [P, 1])
        rstd = sb("rstd", [P, 1])
        mem_ss = sb("mem_ss", [P, 2])
        mem_rstd = sb("mem_rstd", [P, 2])
        hss = sb("hss", [P, 20])
        hrs = sb("hrs", [P, 20])
        lf = sb("lf", [P, 4, AH])
        logf = sb("logf", [P, 2, AH])
        nmax = sb("nmax", [P, UNITS])
        rsum = sb("rsum", [P, UNITS])
        rinv = sb("rinv", [P, UNITS])
        pick = sb("pick", [P, 2, TOPK])
        picki = sb("picki", [P, 2, TOPK], U32)
        pickf = sb("pickf", [P, 2, TOPK])
        ks = sb("ks", [P, 2, 2 * PKEYS])
        left = sb("left", [P, 2, PKEYS])
        mate_hT = pT
        onehot = pr[:, 0:512].rearrange("p (q i j) -> p q i j", q=2, i=TOPK)
        cand = pr[:, 512:768].rearrange("p (i j) -> p i j", i=TOPK)
        candleft = pr[:, 768:1024]
        ci = sb("ci", [P, TOPK], U32)
        cij = sb("cij", [P, 2, TOPK], U32)
        cijf = sb("cijf", [P, 2, TOPK])
        e12 = sb("e12", [P, 2, TOPK])
        sc = sb("sc", [P, PH, TOPK])
        ex = sb("ex", [P, PH, TOPK])
        esum = sb("esum", [P, PH])
        x2n, xtn = x, xn
        idxn = sb("idxn", [P, PH, TOPK], U32)
        gaten = sb("gaten", [P, PH, TOPK])
        xt = sb("xt", [P, D])
        idx = sb("idx", [P, SLOTS], U32)
        gate = sb("gate", [P, PH, TOPK])
        urow = sb("urow", [P, NU, D])
        vrow = sb("vrow", [P, NV, D])
        act = sb("act", [P, PH, TOPK])
        gel = sb("gel", [P, PH, TOPK])
        wgt = sb("wgt", [P, SLOTS])
        diag = sb("diag", [P, ND, P])
        acc2 = sb("acc2", [P, D])

        def ps(name, shape):
            return ctx.enter_context(nc.psum_tensor(name, shape, F32))

        acc = ps("acc", [P, D])
        S = ps("S", [P, SEQ])
        tp = ps("tp", [P, KB, P])
        g = [ps("g0", [P, BANK]), ps("g1", [P, BANK])]

        def sem(name):
            return ctx.enter_context(nc.semaphore(name))

        const_loaded = sem("const_loaded")
        const_made = sem("const_made")
        zeroed = sem("zeroed")
        gains = sem("gains")
        x_loaded = sem("x_loaded")
        xn_ready = sem("xn_ready")
        sq_done = sem("sq_done")
        rms_ready = sem("rms_ready")
        turned = sem("turned")
        hT_ready = sem("hT_ready")
        fl_done = sem("fl_done")
        gemm_done = sem("gemm_done")
        z_ready = sem("z_ready")
        mate_x_loaded = sem("mate_x_loaded")
        mate_f_ready = sem("mate_f_ready")
        mate_gemm_done = sem("mate_gemm_done")
        mate_z_ready = sem("mate_z_ready")
        bcT_ready = sem("bcT_ready")
        qk_squares = sem("qk_squares")
        qk_rms = sem("qk_rms")
        qkn_ready = sem("qkn_ready")
        qk_turned = sem("qk_turned")
        qT_ready = sem("qT_ready")
        kT_ready = sem("kT_ready")
        qm_turned = sem("qm_turned")
        qmT_ready = sem("qmT_ready")
        f_ready = sem("f_ready")
        f_exp = sem("f_exp")
        f_ln = sem("f_ln")
        logf_ready = sem("logf_ready")
        cum_done = sem("cum_done")
        cum_used = sem("cum_used")
        s_done = sem("s_done")
        nmax_ready = sem("nmax_ready")
        exp_done = sem("exp_done")
        p_turned = sem("p_turned")
        pT_ready = sem("pT_ready")
        v_added = sem("v_added")
        pv_done = sem("pv_done")
        mix_ready = sem("mix_ready")
        mix_turned = sem("mix_turned")
        mixT_ready = sem("mixT_ready")
        u_ready = sem("u_ready")
        conv_ready = sem("conv_ready")
        x2_ready = sem("x2_ready")
        sq2_done = sem("sq2_done")
        rms2_ready = sem("rms2_ready")
        xt_ready = sem("xt_ready")
        xt_turned = sem("xt_turned")
        xtT_ready = sem("xtT_ready")
        pqT_ready = sem("pqT_ready")
        key_scores = sem("key_scores")
        picked = sem("picked")
        ks_ready = sem("ks_ready")
        diff_ready = sem("diff_ready")
        ex_ready = sem("ex_ready")
        stored = sem("stored")
        first_picked = sem("first_picked")
        copied = sem("copied")
        idx_spread = sem("idx_spread")
        xt_spread = sem("xt_spread")
        gate_spread = sem("gate_spread")
        acc2_zeroed = sem("acc2_zeroed")
        x2_copied = sem("x2_copied")
        dots = sem("dots")
        gelu_done = sem("gelu_done")
        wgt_ready = sem("wgt_ready")
        diag_ready = sem("diag_ready")
        v_used = sem("v_used")
        y_ready = sem("y_ready")
        y_stored = sem("y_stored")
        dve_chain = sem("dve_chain")
        pool_chain = sem("pool_chain")
        cache_loaded = sem("cache_loaded")
        cache_turned = sem("cache_turned")
        cache_copied = sem("cache_copied")
        ft_done = sem("ft_done")
        ft_used = sem("ft_used")
        mm_loaded = sem("mm_loaded")
        w_loaded = [sem(f"w_loaded{i}") for i in range(NW)]
        u_landed = [sem(f"u_landed{i}") for i in range(NU)]
        v_landed = [sem(f"v_landed{i}") for i in range(NV)]
        first, last = const_loaded.num, v_landed[NV - 1].num
        every_semaphore = range(first, last + 1)
        assert len(every_semaphore) == 79 + NW + NU + NV

        def end_block():
            nc.all_engine_barrier(sems_to_clear=every_semaphore)

        def load_chunk(sp, c, n, src):
            i = n - c.chunk0
            if i >= NW:
                sp.wait_ge(gemm_done, i - NW + 1)
                if c.mate is not None:
                    sp.wait_ge(mate_gemm_done, min(n - NW + 1, 10))
            sp.dma_start(wbuf[:, i % NW, :, :], src.rearrange("(k p) n -> p k n", p=P)).then_inc(w_loaded[i % NW], 16)

        def heads_of(ap, n):
            return ap.rearrange("p (h d) -> p h d", h=n)

        def setup():
            mem_x, mem_xn, mem_hT = (x, acc2), (xn, xt), (hT, mate_hT)
            mem_keys = [mate_z[:, i * 2 * MW:i * 2 * MW + MW] for i in range(2)]
            mem_raw = [mate_z[:, i * 2 * MW + MW:(i + 1) * 2 * MW] for i in range(2)]

            with nc.Block() as block:
                @block.sync
                def _(sp):
                    sp.dma_start(mem_x[0][:, :], d_mem_prompt[0][0:P, :]).then_inc(x_loaded, 16)
                    sp.dma_start(mem_x[1][:, :], d_mem_prompt[0][P:2 * P, :]).then_inc(mate_x_loaded, 16)
                    sp.dma_start(wbuf[:, 0, :, 0:MW], d_w_mem_k[0].rearrange("(k p) n -> p k n", p=P)).then_inc(mm_loaded, 16)
                    sp.dma_start(wbuf[:, 1, :, :], d_w_mem_v[0].rearrange("(k p) n -> p k n", p=P)).then_inc(mm_loaded, 16)
                    loads = [(g_attn[:, :], d_g_attn[0].rearrange("(k p) -> p k", p=P)),
                             (g_mem[:, :], d_g_mem[0].rearrange("(k p) -> p k", p=P)),
                             (g_ffn[:, :], d_g_ffn[0].partition_broadcast(P)),
                             (g_q[:, :], d_g_q_a[0].partition_broadcast(P)),
                             (g_k[:, :], d_g_k_a[0].partition_broadcast(P)),
                             (g_qm[:, :], d_g_q_m[0].partition_broadcast(P)),
                             (g_km[:, :], d_g_k_m[0].partition_broadcast(P)),
                             (bias_f[:, :], d_b_f[0].partition_broadcast(P)),
                             (w_f[:, :, :], d_w_in[0][:, FCOL:BCOL].rearrange("(k p) n -> p k n", p=P))]
                    for j in range(3):
                        loads.append((conv_w[:, :, j], d_conv_w[0][j].rearrange("(b p) -> p b", p=P)))
                    loads.append((conv_b[:, :], d_conv_b[0].rearrange("(b p) -> p b", p=P)))
                    with nc.allow_non_contiguous_dma("vectors laid along partitions, once"):
                        for dst, src in loads:
                            sp.dma_start(dst, src).then_inc(const_loaded, 16)
                    sp.dma_start(z[:, 0:D].rearrange("p (g d) -> p g d", d=HD),
                                 d_peer_keys[0].rearrange("h q k d -> k (h q) d")).then_inc(cache_loaded, 16)
                    for i in range(2):
                        sp.wait_ge(qkn_ready, i + 1)
                        sp.dma_start(d_m_k[0][0][i * P:(i + 1) * P].rearrange("n h d -> n (h d)"), mem_keys[i]).then_inc(stored, 16)
                        sp.dma_start(d_m_v[0][0][i * P:(i + 1) * P].rearrange("n h d -> n (h d)"), mv[:, i, :]).then_inc(stored, 16)
                    sp.wait_ge(stored, 64)
                    sp.wait_ge(const_loaded, 16 * len(loads))

                @block.gpsimd
                def _(pool):
                    chain = Chain(pool, pool_chain)
                    chain.do(pool.memset(ident[:, :], 0.0))
                    chain.do(pool.affine_select(ident[:, :], ident[:, :], [[-1, P]], ALU.not_equal, 1.0, base=0, channel_multiplier=1))
                    chain.do(pool.memset(upto[:, :], 1.0))
                    chain.do(pool.affine_select(upto[:, :], upto[:, :], [[1, P]], ALU.is_ge, 0.0, base=0, channel_multiplier=-1))
                    chain.do(pool.memset(causal[:, :], 0.0))
                    chain.do(pool.affine_select(causal[:, :], causal[:, :], [[-1, P]], ALU.is_ge, NEG, base=0, channel_multiplier=1))
                    chain.do(pool.memset(headrow[:, :, :], 0.0))
                    chain.do(pool.affine_select(headrow[:, :, :], headrow[:, :, :], [[-1, AH], [0, P]], ALU.not_equal, 1.0, base=0, channel_multiplier=1))
                    chain.do(pool.tensor_copy(fold[:, :], ident[:, 0:NEW]))
                    for i in range(1, P // NEW):
                        chain.do(pool.tensor_tensor(fold[:, :], fold[:, :], ident[:, i * NEW:(i + 1) * NEW], ALU.add))
                    for cleared in (kT[:, :, :], v_all[:, :, :], qT[:, :, :], uT[:, :, :], ncarry[:, :]):
                        pool.memset(cleared, 0.0).then_inc(zeroed, 1)
                    pool.iota(iota16[:, :], [[1, TOPK]], base=0, channel_multiplier=0,
                              allow_small_or_imprecise_dtypes=True).then_inc(const_made, 1)

                @block.vector
                def _(v):
                    chain = Chain(v, dve_chain)
                    chain.do(v.memset(negF[:, :], 0.0))
                    v.memset(negF[0:AH, :], NEG).then_inc(zeroed, 1)
                    chain.do(v.memset(keys2[:, :, :], 0.0))
                    for i in range(2):
                        v.wait_ge(sq_done, i + 1)
                        v.tensor_scalar(mem_ss[:, i:i + 1], mem_ss[:, i:i + 1], 1.0 / D, EPS, ALU.mult, ALU.add).then_inc(rms_ready, 1)
                    for i in range(2):
                        v.wait_ge(rms2_ready, i + 1)
                        chain.do(v.reciprocal(mem_rstd[:, i:i + 1], mem_ss[:, i:i + 1]))
                        v.tensor_scalar(mem_xn[i][:, :], mem_x[i][:, :], mem_rstd[:, i:i + 1], None, ALU.mult).then_inc(xn_ready, 1)
                    v.wait_ge(const_loaded, 16 * 13)
                    v.tensor_scalar(g_q[:, :], g_q[:, :], HD ** -0.5, None, ALU.mult).then_inc(gains, 1)
                    v.tensor_scalar(g_qm[:, :], g_qm[:, :], HD ** -0.5, None, ALU.mult).then_inc(gains, 1)
                    for i in range(2):
                        v.wait_ge(turned, i + 1)
                        v.tensor_tensor(mem_hT[i][:, :, :], tp[:, :, :], g_mem[:, :].unsqueeze(2).to_broadcast([P, KB, P]),
                                        ALU.mult).then_inc(hT_ready, 1)
                    v.wait_ge(cache_turned, 1)
                    v.tensor_copy(keys2[0:HD, :, 0:PKEYS], tp[0:HD, :, :]).then_inc(cache_copied, 1)
                    v.tensor_copy(keys2[HD:P, :, PKEYS:2 * PKEYS], tp[HD:P, :, :]).then_inc(cache_copied, 1)
                    for i in range(2):
                        v.wait_ge(gemm_done, i + 1)
                        keys, raw = heads_of(mem_keys[i], MH), heads_of(mem_raw[i], MH)
                        sums, roots = hss[:, i * MH:(i + 1) * MH], hrs[:, i * MH:(i + 1) * MH]
                        chain.do(v.tensor_copy(mv[:, i, :], g[i][:, MW:2 * MW]))
                        chain.do(v.tensor_copy(mem_raw[i], g[i][:, 0:MW]))
                        chain.do(v.tensor_tensor(mem_keys[i], mem_raw[i], mem_raw[i], ALU.mult))
                        chain.do(v.tensor_reduce(sums, keys, AX, ALU.add))
                        v.tensor_scalar(sums, sums, 1.0 / HD, EPS, ALU.mult, ALU.add).then_inc(qk_squares, 1)
                        v.wait_ge(qk_rms, i + 1)
                        chain.do(v.reciprocal(roots, sums))
                        chain.do(v.tensor_tensor(keys, raw, roots.unsqueeze(2).to_broadcast([P, MH, HD]), ALU.mult))
                        v.tensor_tensor(keys, keys, g_km[:, :].unsqueeze(1).to_broadcast([P, MH, HD]), ALU.mult).then_inc(qkn_ready, 1)
                    for i in range(2):
                        v.wait_ge(qk_turned, i + 1)
                        v.tensor_copy(mkT[:, :, i * P:(i + 1) * P], S[:, i * BANK:i * BANK + MW].rearrange("p (a b) -> p a b", a=2)).then_inc(kT_ready, 1)

                @block.scalar
                def _(act_):
                    for i, loaded in enumerate((x_loaded, mate_x_loaded)):
                        act_.wait_ge(loaded, 16)
                        if i:
                            act_.wait_ge(sq_done, 1)
                        act_.activation(pr[:, :], mem_x[i][:, :], ACT.Square, accum_out=mem_ss[:, i:i + 1]).then_inc(sq_done, 1)
                    for i in range(2):
                        act_.wait_ge(rms_ready, i + 1)
                        act_.activation(mem_ss[:, i:i + 1], mem_ss[:, i:i + 1], ACT.Sqrt).then_inc(rms2_ready, 1)
                    for i in range(2):
                        act_.wait_ge(qk_squares, i + 1)
                        act_.activation(hss[:, i * MH:(i + 1) * MH], hss[:, i * MH:(i + 1) * MH], ACT.Sqrt).then_inc(qk_rms, 1)

                @block.tensor
                def _(pe):
                    pe.wait_ge(const_made, 1)
                    for i in range(2):
                        pe.wait_ge(xn_ready, i + 1)
                        if i:
                            pe.wait_ge(hT_ready, 1)
                        for k in range(KB):
                            last = pe.transpose(tp[:, k, :], mem_xn[i][:, k * P:(k + 1) * P], ident[:, :])
                        last.then_inc(turned, 1)
                    pe.wait_ge(mm_loaded, 32)
                    for i in range(2):
                        pe.wait_ge(hT_ready, i + 1)
                        for k in range(KB):
                            pe.matmul(g[i][:, 0:MW], mem_hT[i][:, k, :], wbuf[:, 0, k, :], start=k == 0, stop=k == KB - 1)
                        for k in range(KB):
                            last = pe.matmul(g[i][:, MW:2 * MW], mem_hT[i][:, k, :], wbuf[:, 1, k, :], start=k == 0, stop=k == KB - 1)
                        last.then_inc(gemm_done, 1)
                        if i == 0:
                            pe.wait_ge(cache_loaded, 16)
                            pe.wait_ge(hT_ready, 2)
                            for h in range(PH):
                                last = pe.transpose(tp[:, h, :], z[:, h * P:(h + 1) * P], ident[:, :])
                            last.then_inc(cache_turned, 1)
                    for i in range(2):
                        pe.wait_ge(qkn_ready, i + 1)
                        for k in range(2):
                            last = pe.transpose(S[:, i * BANK + k * P:i * BANK + (k + 1) * P], mem_keys[i][:, k * P:(k + 1) * P], ident[:, :])
                        last.then_inc(qk_turned, 1)
            end_block()


        def prepare_sync(sp, e, c):
            R = c.rows
            if e is not None:
                sp.wait_ge(x2_copied, 1)
            sp.dma_start(x[:R, :], c.x_in).then_inc(x_loaded, 16)
            if c.mate is not None:
                sp.dma_start(mate_z[:c.mate.rows, 0:D], c.mate.x_in).then_inc(mate_x_loaded, 16)
            if c.sample:
                sp.wait_ge(copied, 1)
                sp.dma_start(v_all[:, 0:2, :], d_cache_a_v[0][0].rearrange("(b p) h d -> p b (h d)", p=P)).then_inc(cache_loaded, 16)
                sp.dma_start(mv[:, :, :], d_cache_m_v[0][0].rearrange("(b p) h d -> p b (h d)", p=P)).then_inc(cache_loaded, 16)
                for b in range(2):
                    sp.dma_start(logf[:, b, :], d_cache_a_logf[0][0][b * P:(b + 1) * P, :]).then_inc(cache_loaded, 16)
                    sp.dma_start(z[:, b * AW:(b + 1) * AW], d_cache_a_k[0][0][b * P:(b + 1) * P].rearrange("p h d -> p (h d)")).then_inc(cache_loaded, 16)
                    sp.dma_start(xn[:, b * MW:(b + 1) * MW], d_cache_m_k[0][0][b * P:(b + 1) * P].rearrange("p h d -> p (h d)")).then_inc(cache_loaded, 16)
                    with nc.allow_non_contiguous_dma("2 rows of history, channels to partitions"):
                        sp.dma_start(uT[:, b, 0:2], d_cache_b_conv[0][0][:, b * P:(b + 1) * P].rearrange("t c -> c t")).then_inc(cache_loaded, 16)
            w_in, w_out, w_pq = d_w_in[0], d_w_out[0], d_w_peer_q[0]
            cols = [w_in[:, i * CHUNK:(i + 1) * CHUNK] for i in range(6)] + [w_in[:, BCOL + i * CHUNK:BCOL + (i + 1) * CHUNK] for i in range(4)]
            cols += [w[:, i * CHUNK:(i + 1) * CHUNK] for w in (w_out, w_pq) for i in range(4)]
            for n in range(c.chunk0, 10):
                load_chunk(sp, c, n, cols[n])
            if c.kind != SECOND:
                sp.wait_ge(z_ready, 3)
            own_z = mate_z if c.kind == SECOND else z
            sp.dma_start(c.v_out, own_z[:R, 2 * AW:3 * AW]).then_inc(stored, 16)
            sp.wait_ge(qkn_ready, 2)
            sp.dma_start(c.k_out, own_z[:R, AW:2 * AW]).then_inc(stored, 16)
            sp.wait_ge(logf_ready, 1)
            sp.dma_start(c.logf_out, lf[:R, 0, :]).then_inc(stored, 16)
            sp.wait_ge(u_ready, 1)
            for b in range(2):
                with nc.allow_non_contiguous_dma("2 rows of convolution state, channels on partitions"):
                    sp.dma_start(c.conv_out[:, b * P:(b + 1) * P].rearrange("t c -> c t"), uT[:, b, R:R + 2]).then_inc(stored, 16)
            for n in range(10, 18):
                load_chunk(sp, c, n, cols[n])
            sp.wait_ge(stored, 16 * 5)

        def prepare_tensor(pe, c):
            R, W = c.rows, c.blocks * P

            def chunk_ready(n):
                i = n - c.chunk0
                pe.wait_ge(w_loaded[i % NW], 16 * (i // NW + 1))
                return wbuf[:, i % NW]

            def rows_by_columns(n, out, rowsT, signal):
                w = chunk_ready(n)
                for k in range(KB):
                    last = pe.matmul(out, rowsT[:, k, :], w[:, k, :], start=k == 0, stop=k == KB - 1)
                last.then_inc(signal, 1)

            def columns_by_rows(n, bank, at, rowsT, signal):
                w, rows = chunk_ready(n), rowsT.shape[-1]
                for j in range(CHUNK // P):
                    for k in range(KB):
                        last = pe.matmul(bank[:, (at + j) * P:(at + j) * P + rows], w[:, k, j * P:(j + 1) * P], rowsT[:, k, :],
                                         start=k == 0, stop=k == KB - 1)
                last.then_inc(signal, 1)

            def input_chunk(n, banks, rowsT, rows, copied_out, signal):
                if n < 6:
                    if n == 4:
                        pe.wait_ge(copied_out, 1)
                    rows_by_columns(n, banks[n // 2 % 2][:rows, n % 2 * CHUNK:(n % 2 + 1) * CHUNK], rowsT, signal)
                elif n < 8:
                    pe.wait_ge(copied_out, 2)
                    columns_by_rows(n, banks[1], n % 2 * 2, rowsT, signal)
                elif n == 8:
                    pe.wait_ge(copied_out, 3)
                    columns_by_rows(8, banks[0], 0, rowsT, signal)
                else:
                    rows_by_columns(9, banks[0][:rows, CHUNK:BANK], rowsT, signal)

            def forget_logits(block, rowsT):
                rows = rowsT.shape[-1]
                for k in range(KB):
                    last = pe.matmul(tp[:rows, block, 0:AH], rowsT[:, k, :], w_f[:, k, :], start=k == 0, stop=k == KB - 1)
                last.then_inc(fl_done, 1)

            def turn(dst, src, width, signal, rows=R):
                for k in range(width // P):
                    last = pe.transpose(tp[:, dst + k, :rows], src[:rows, k * P:(k + 1) * P], ident[:rows, :rows])
                last.then_inc(signal, 1)

            own_z = mate_z if c.kind == SECOND else z
            own_hT = hT[:, :, :R]
            yield "square"
            if c.sample:
                pe.wait_ge(cache_loaded, 16 * 10)
                for b in range(2):
                    if b:
                        pe.wait_ge(cache_copied, 1)
                    for k in range(4):
                        pe.transpose(tp[:, k, :], z[:, b * AW + k * P:b * AW + (k + 1) * P], ident[:, :])
                    for k in range(2):
                        last = pe.transpose(tp[:, 4 + k, :], xn[:, b * MW + k * P:b * MW + (k + 1) * P], ident[:, :])
                    last.then_inc(cache_turned, 1)
                for b in range(2):
                    if b:
                        pe.wait_ge(ft_used, 1)
                    pe.matmul(g[0][0:AH, 0:P], logf[:, b, :], upto[:, :], start=True, stop=True).then_inc(ft_done, 1)
                pe.wait_ge(cache_copied, 2)
                pe.wait_ge(ft_used, 2)
            if c.kind != SECOND:
                yield "turn"
                pe.wait_ge(xn_ready, 1)
                turn(0, xn, D, turned)
                if c.mate is not None:
                    yield "mate_turn"
                    pe.wait_ge(xn_ready, 2)
                    pe.wait_ge(hT_ready, 1)
                    turn(0, xn, D, turned, c.mate.rows)
                for n in range(10):
                    yield f"w{n}"
                    if n == 0:
                        pe.wait_ge(hT_ready, 1)
                        if c.mate is not None:
                            pe.wait_ge(hT_ready, 2)
                        forget_logits(0, own_hT)
                    input_chunk(n, g, own_hT, R, z_ready, gemm_done)
                    if c.mate is not None:
                        yield f"mate{n}"
                        its_hT = mate_hT[:, :, :c.mate.rows]
                        if n == 0:
                            forget_logits(4, its_hT)
                        input_chunk(n, [S[:, 0:BANK], S[:, BANK:2 * BANK]], its_hT, c.mate.rows, mate_z_ready, mate_gemm_done)
            yield "headsq"
            pe.wait_ge(logf_ready, 1)
            if c.kind != SECOND:
                pe.wait_ge(bcT_ready, 1)
            pe.matmul(g[1][0:AH, 0:R], lf[:R, 0, :], upto[:R, :R], start=True, stop=True).then_inc(cum_done, 1)
            yield "turnqk"
            pe.wait_ge(f_ready, 1)
            if c.mate is not None:
                pe.wait_ge(mate_f_ready, 1)
            pe.wait_ge(qkn_ready, 3)
            turn(0, own_z, 2 * AW, qk_turned)
            yield "turnqm"
            pe.wait_ge(qT_ready, 2)
            turn(0, own_z[:, 3 * AW:], MW, qm_turned)

            def scores(n):
                if n < AH:
                    for lo in range(0, W, BANK):
                        hi = min(lo + BANK, W)
                        pe.matmul(S[:R, lo:hi], qT[:, n, :R], kT[:, n // 2, lo:hi], start=True, stop=False)
                    pe.matmul(c.own_keys(S)[:R], ident[:R, :R], causal[:R, :R], start=False, stop=False)
                    for lo in range(0, W, BANK):
                        hi = min(lo + BANK, W)
                        last = pe.matmul(S[:R, lo:hi], headrow[:, n, :R], negF[:, lo:hi], start=False, stop=True)
                else:
                    last = pe.matmul(S[:R, 0:NMEM], qT[:, n, :R], mkT[:, (n - AH) // 2, :], start=True, stop=True)
                last.then_inc(s_done, 1)

            def blocks(n):
                return c.blocks if n < AH else NMEM // P

            def key_scores_of(h):
                pe.wait_ge(pqT_ready, h // 4 + 1)
                if h >= 2:
                    pe.wait_ge(ks_ready, h - 1)
                pe.matmul(S[:R, (h % 2) * BANK:(h % 2) * BANK + 2 * PKEYS], pT[:, h, :R], keys2[:, h, :], start=True, stop=True).then_inc(key_scores, 1)

            yield "att0a"
            pe.wait_ge(kT_ready, 1)
            pe.wait_ge(qmT_ready, 2)
            pe.wait_ge(cum_used, 1)
            if c.mate is not None:
                pe.wait_ge(mate_z_ready, 6)
            scores(0)
            for n in range(1, UNITS + 1):
                m = n - 1
                yield f"att{n}a"
                pe.wait_ge(exp_done, n)
                if m:
                    pe.wait_ge(pT_ready, m)
                turn(0, pr, blocks(m) * P, p_turned)
                if n < UNITS:
                    scores(n)
                yield f"att{n}c"
                pe.wait_ge(pT_ready, n)
                for b in range(blocks(m)):
                    if m < AH:
                        out, val = g[0][:R, m * HD:(m + 1) * HD], v_all[:, b, m * HD:(m + 1) * HD]
                    else:
                        out, val = g[1][:R, (m - AH) * HD:(m - AH + 1) * HD], mv[:, b, (m - AH) * HD:(m - AH + 1) * HD]
                    last = pe.matmul(out, pT[:, b, :R], val, start=b == 0, stop=b == blocks(m) - 1)
                last.then_inc(pv_done, 1)
            yield "turnmix"
            pe.wait_ge(mix_ready, 2)
            turn(0, xn, AW + MW, mix_turned)
            for n in range(10, 14):
                yield f"w{n}"
                if n == 10:
                    pe.wait_ge(mixT_ready, 2)
                    pe.wait_ge(conv_ready, 2)
                rows_by_columns(n, S[:R, (n - 10) * CHUNK:(n - 9) * CHUNK], own_hT, gemm_done)
            yield "turn2"
            pe.wait_ge(xt_ready, 1)
            turn(0, xtn, D, xt_turned)
            for n in range(14, 18):
                yield f"w{n}"
                if n == 14:
                    pe.wait_ge(xtT_ready, 1)
                if n == 16:
                    key_scores_of(0)
                    key_scores_of(1)
                columns_by_rows(n, g[(n - 14) // 2], n % 2 * 2, own_hT, gemm_done)
            for h in range(2, PH):
                yield f"top{h - 1}"
                key_scores_of(h)

        def prepare_scalar(sc_, c):
            R, W = c.rows, c.blocks * P

            def copy(dst, src, signal):
                sc_.activation(dst, src, ACT.Copy).then_inc(signal, 1)

            its = c.mate.rows if c.mate is not None else None
            if c.kind != SECOND:
                yield "square"
                sc_.wait_ge(x_loaded, 16)
                sc_.activation(pr[:R, :], x[:R, :], ACT.Square, accum_out=ss[:R, :]).then_inc(sq_done, 1)
                yield "root"
                sc_.wait_ge(rms_ready, 1)
                sc_.activation(ss[:R, :], ss[:R, :], ACT.Sqrt).then_inc(rms_ready, 1)
                if its:
                    yield "mate_square"
                    sc_.wait_ge(mate_x_loaded, 16)
                    sc_.wait_ge(xn_ready, 1)
                    sc_.activation(pr[:its, :], mate_z[:its, 0:D], ACT.Square, accum_out=ss[:its, :]).then_inc(sq_done, 1)
                    yield "mate_root"
                    sc_.wait_ge(rms_ready, 3)
                    sc_.activation(ss[:its, :], ss[:its, :], ACT.Sqrt).then_inc(rms_ready, 1)
                for n in range(3):
                    yield f"w{2 * n + 2}"
                    sc_.wait_ge(gemm_done, 2 * n + 2)
                    copy(z[:R, n * AW:(n + 1) * AW], g[n % 2][:R, :], z_ready)
                    if its:
                        yield f"mate{2 * n + 2}"
                        sc_.wait_ge(mate_gemm_done, 2 * n + 2)
                        copy(mate_z[:its, n * AW:(n + 1) * AW], S[:its, n % 2 * BANK:(n % 2 + 1) * BANK], mate_z_ready)
                sc_.wait_ge(z_ready, 3)
                copy(c.own_values, z[:R, 2 * AW:3 * AW], kT_ready)
            else:
                yield "w6"
                copy(c.own_values, mate_z[:R, 2 * AW:3 * AW], kT_ready)
            sc_.wait_ge(f_ready, 1)
            sc_.activation(lf[:R, 2, :], lf[:R, 1, :], ACT.Exp).then_inc(f_exp, 1)
            sc_.wait_ge(f_exp, 1)
            sc_.activation(lf[:R, 3, :], lf[:R, 2, :], ACT.Ln, bias=1.0).then_inc(f_ln, 1)
            if c.kind != SECOND:
                def blocks_of(bank, n, rows):
                    return bank[:, 0:n * P].rearrange("p (j q) -> p j q", j=n)[:, :, :rows]

                yield "w8"
                sc_.wait_ge(gemm_done, 8)
                copy(bcT[:, :, :R], blocks_of(g[1], 4, R), bcT_ready)
                if its:
                    yield "mate8"
                    sc_.wait_ge(mate_gemm_done, 8)
                    copy(mate_bcT[:, 0:4, :its], blocks_of(S[:, BANK:2 * BANK], 4, its), mate_z_ready)
                yield "qm"
                sc_.wait_ge(gemm_done, 10)
                copy(z[:R, 3 * AW:3 * AW + MW], g[0][:R, MW:2 * MW], z_ready)
                if its:
                    sc_.wait_ge(mate_gemm_done, 10)
                    copy(mate_z[:its, 3 * AW:3 * AW + MW], S[:its, MW:2 * MW], mate_z_ready)
                    copy(mate_bcT[:, 4:6, :its], blocks_of(S[:, 0:BANK], 2, its), mate_z_ready)
            yield "headroot"
            sc_.wait_ge(qk_squares, 1)
            sc_.activation(hss[:R, :], hss[:R, :], ACT.Sqrt).then_inc(qk_rms, 1)
            for n in range(UNITS + 1):
                yield f"att{n}b"
                if n:
                    m = n - 1
                    nb = c.blocks if m < AH else NMEM // P
                    sc_.wait_ge(p_turned, n)
                    if m:
                        sc_.wait_ge(pv_done, m)
                    copy(pT[:, 0:nb, :R], tp[:, 0:nb, :R], pT_ready)
                if n < UNITS:
                    yield f"att{n}c"
                    w = W if n < AH else NMEM
                    sc_.wait_ge(nmax_ready, n + 1)
                    sc_.activation(pr[:R, 0:w], S[:R, 0:w], ACT.Exp, bias=nmax[:R, n:n + 1], accum_out=rsum[:R, n:n + 1]).then_inc(exp_done, 1)
            yield "mixT"
            sc_.wait_ge(mix_turned, 1)
            copy(mixT[:, 0:4, :R], tp[:, 0:4, :R], mixT_ready)
            copy(mixT[:, 6:8, :R], tp[:, 4:6, :R], mixT_ready)
            yield "square2"
            sc_.wait_ge(x2_ready, 1)
            sc_.activation(pr[:R, :], x2n[:R, :], ACT.Square, accum_out=ss[:R, :]).then_inc(sq2_done, 1)
            yield "root2"
            sc_.wait_ge(rms2_ready, 1)
            sc_.activation(ss[:R, :], ss[:R, :], ACT.Sqrt).then_inc(rms2_ready, 1)
            yield "xtT"
            sc_.wait_ge(xt_turned, 1)
            copy(hT[:, :, :R], tp[:, :, :R], xtT_ready)
            def expert_queries(i):
                sc_.wait_ge(gemm_done, 16 + 2 * i - c.chunk0)
                copy(pT[:, 4 * i:4 * i + 4, :R], g[i][:, :].rearrange("p (j q) -> p j q", j=4)[:, :, :R], pqT_ready)

            def scores_out(h):
                sc_.wait_ge(key_scores, h + 1)
                if h >= 2:
                    sc_.wait_ge(picked, h - 1)
                copy(ks[:R, h % 2, :], S[:R, (h % 2) * BANK:(h % 2) * BANK + 2 * PKEYS], ks_ready)

            yield "w16"
            expert_queries(0)
            yield "w17"
            scores_out(0)
            scores_out(1)
            yield "pqT"
            expert_queries(1)
            for h in range(2, PH):
                yield f"top{h}"
                scores_out(h)
            yield "gate1"
            sc_.wait_ge(diff_ready, 1)
            sc_.activation(ex[:R, :, :], ex[:R, :, :], ACT.Exp).then_inc(ex_ready, 1)

        def prepare_vector(v, c, chain):
            R, W = c.rows, c.blocks * P
            do = chain.do
            if c.sample:
                yield "cache"
                for b in range(2):
                    v.wait_ge(cache_turned, b + 1)
                    do(v.tensor_copy(kT[:, :, b * P:(b + 1) * P], tp[:, 0:4, :]))
                    v.tensor_copy(mkT[:, :, b * P:(b + 1) * P], tp[:, 4:6, :]).then_inc(cache_copied, 1)
                do(v.memset(negF[0:AH, PAST:PAST + P], NEG))
                do(v.memset(ncarry[:, :], 0.0))
                for b in range(2):
                    v.wait_ge(ft_done, b + 1)
                    do(v.tensor_scalar(negF[0:AH, b * P:(b + 1) * P], g[0][0:AH, 0:P], -1.0, ncarry[:, 0:1], ALU.mult, ALU.add))
                    v.tensor_scalar(ncarry[:, :], g[0][0:AH, P - 1:P], -1.0, ncarry[:, 0:1], ALU.mult, ALU.add).then_inc(ft_used, 1)
                    v.wait_ge(ft_used, b + 1)
                v.wait_ge(cache_loaded, 16 * 10)
            own_z = mate_z if c.kind == SECOND else z
            if c.kind != SECOND:
                yield "rms"
                v.wait_ge(sq_done, 1)
                v.tensor_scalar(ss[:R, :], ss[:R, :], 1.0 / D, EPS, ALU.mult, ALU.add).then_inc(rms_ready, 1)
                yield "scale"
                v.wait_ge(rms_ready, 2)
                do(v.reciprocal(rstd[:R, :], ss[:R, :]))
                v.tensor_scalar(xn[:R, :], x[:R, :], rstd[:R, 0:1], None, ALU.mult).then_inc(xn_ready, 1)
                yield "hT"
                v.wait_ge(turned, 1)
                v.tensor_tensor(hT[:, :, :R], tp[:, :, :R], g_attn[:, :].unsqueeze(2).to_broadcast([P, KB, R]), ALU.mult).then_inc(hT_ready, 1)
                if c.mate is not None:
                    its = c.mate.rows
                    yield "mate_rms"
                    v.wait_ge(sq_done, 2)
                    v.tensor_scalar(ss[:its, :], ss[:its, :], 1.0 / D, EPS, ALU.mult, ALU.add).then_inc(rms_ready, 1)
                    yield "mate_scale"
                    v.wait_ge(rms_ready, 4)
                    do(v.reciprocal(rstd[:its, :], ss[:its, :]))
                    v.tensor_scalar(xn[:its, :], mate_z[:its, 0:D], rstd[:its, 0:1], None, ALU.mult).then_inc(xn_ready, 1)
                    yield "mate_hT"
                    v.wait_ge(turned, 2)
                    v.tensor_tensor(mate_hT[:, :, :its], tp[:, :, :its], g_attn[:, :].unsqueeze(2).to_broadcast([P, KB, its]), ALU.mult).then_inc(hT_ready, 1)
            yield "w1"
            if c.kind != SECOND:
                v.wait_ge(fl_done, 1)
                do(v.tensor_tensor(lf[:R, 0, :], tp[:R, 0, 0:AH], bias_f[:R, :], ALU.add))
                if c.mate is not None:
                    yield "mate1"
                    v.wait_ge(fl_done, 2)
                    v.tensor_tensor(mate_f[:its, :], tp[:its, 4, 0:AH], bias_f[:its, :], ALU.add).then_inc(mate_f_ready, 1)
            else:
                do(v.tensor_copy(lf[:R, 0, :], mate_f[:R, :]))
            do(v.tensor_scalar(lf[:R, 1, :], lf[:R, 0, :], -1.0, None, ALU.mult))
            v.tensor_tensor(lf[:R, 1, :], lf[:R, 1, :], lf[:R, 0, :], ALU.min).then_inc(f_ready, 1)
            yield "w7"
            v.wait_ge(f_ln, 1)
            do(v.tensor_scalar(lf[:R, 0, :], lf[:R, 0, :], 0.0, None, ALU.min))
            v.tensor_tensor(lf[:R, 0, :], lf[:R, 0, :], lf[:R, 3, :], ALU.subtract).then_inc(logf_ready, 1)
            yield "conv"
            own_bcT = mate_bcT if c.kind == SECOND else bcT
            if c.kind != SECOND:
                v.wait_ge(gemm_done, 10)
                v.wait_ge(bcT_ready, 1)
                v.wait_ge(z_ready, 4)
                own_h = g[0][:, 0:2 * P].rearrange("p (j q) -> p j q", j=2)
            else:
                own_h = mate_bcT[:, 4:6, :]
            v.tensor_tensor(uT[:, :, 2:2 + R], own_bcT[:, 2:4, :R], own_h[:, :, :R], ALU.mult).then_inc(u_ready, 1)
            v.wait_ge(u_ready, 1)
            for b in range(2):
                do(v.tensor_scalar(yT[:, b, :R], uT[:, b, 2:2 + R], conv_w[:, b, 2:3], conv_b[:, b:b + 1], ALU.mult, ALU.add))
                for j in range(2):
                    do(v.scalar_tensor_tensor(yT[:, b, :R], uT[:, b, j:j + R], conv_w[:, b, j:j + 1], yT[:, b, :R], ALU.mult, ALU.add))
                v.tensor_tensor(mixT[:, 4 + b, :R], yT[:, b, :R], own_bcT[:, b, :R], ALU.mult).then_inc(conv_ready, 1)
            yield "headsq"
            if c.kind != SECOND:
                v.wait_ge(z_ready, 4)
            do(v.tensor_tensor(pr[:R, :], own_z[:R, 0:2 * AW], own_z[:R, 0:2 * AW], ALU.mult))
            do(v.tensor_reduce(hss[:R, 0:16], heads_of(pr[:R, :], 16), AX, ALU.add))
            do(v.tensor_tensor(pr[:R, 0:MW], own_z[:R, 3 * AW:3 * AW + MW], own_z[:R, 3 * AW:3 * AW + MW], ALU.mult))
            do(v.tensor_reduce(hss[:R, 16:20], heads_of(pr[:R, 0:MW], MH), AX, ALU.add))
            v.tensor_scalar(hss[:R, :], hss[:R, :], 1.0 / HD, EPS, ALU.mult, ALU.add).then_inc(qk_squares, 1)
            yield "headnorm"
            v.wait_ge(qk_rms, 1)
            do(v.reciprocal(hrs[:R, :], hss[:R, :]))
            for lo, h0, nh, gain in ((0, 0, AH, g_q), (AW, AH, AH, g_k), (3 * AW, 2 * AH, MH, g_qm)):
                zz = heads_of(own_z[:R, lo:lo + nh * HD], nh)
                do(v.tensor_tensor(zz, zz, hrs[:R, h0:h0 + nh].unsqueeze(2).to_broadcast([R, nh, HD]), ALU.mult))
                v.tensor_tensor(zz, zz, gain[:R, :].unsqueeze(1).to_broadcast([R, nh, HD]), ALU.mult).then_inc(qkn_ready, 1)
            v.wait_ge(cum_done, 1)
            do(v.tensor_scalar(c.own_negF, g[1][0:AH, 0:R], -1.0, ncarry[:, 0:1], ALU.mult, ALU.add))
            v.tensor_scalar(ncarry[:, :], g[1][0:AH, R - 1:R], -1.0, ncarry[:, 0:1], ALU.mult, ALU.add).then_inc(cum_used, 1)
            yield "qT"
            v.wait_ge(qk_turned, 1)
            v.tensor_copy(qT[0:HD, 0:AH:2, :R], tp[0:HD, 0:4, :R]).then_inc(qT_ready, 1)
            v.tensor_copy(qT[HD:P, 1:AH:2, :R], tp[HD:P, 0:4, :R]).then_inc(qT_ready, 1)
            do(v.tensor_copy(c.own_keysT, tp[:, 4:8, :R]))
            yield "qmT"
            v.wait_ge(qm_turned, 1)
            v.tensor_copy(qT[0:HD, AH:UNITS:2, :R], tp[0:HD, 0:2, :R]).then_inc(qmT_ready, 1)
            v.tensor_copy(qT[HD:P, AH + 1:UNITS:2, :R], tp[HD:P, 0:2, :R]).then_inc(qmT_ready, 1)
            for n in range(UNITS):
                yield f"att{n}b"
                v.wait_ge(s_done, n + 1)
                v.tensor_reduce(nmax[:R, n:n + 1], S[:R, 0:W if n < AH else NMEM], AX, ALU.max, negate=True).then_inc(nmax_ready, 1)
            yield "mix"
            v.wait_ge(exp_done, UNITS)
            do(v.reciprocal(rinv[:R, :], rsum[:R, :]))
            v.wait_ge(pv_done, UNITS)
            v.tensor_tensor(heads_of(xn[:R, 0:AW], AH), heads_of(g[0][:R, :], AH), rinv[:R, 0:AH].unsqueeze(2).to_broadcast([R, AH, HD]), ALU.mult).then_inc(mix_ready, 1)
            v.tensor_tensor(heads_of(xn[:R, AW:AW + MW], MH), heads_of(g[1][:R, 0:MW], MH), rinv[:R, AH:UNITS].unsqueeze(2).to_broadcast([R, MH, HD]), ALU.mult).then_inc(mix_ready, 1)
            v.wait_ge(conv_ready, 2)
            v.wait_ge(stored, 16 * 5)
            do(v.tensor_copy(uT[:, :, 0:2], uT[:, :, R:R + 2]))
            yield "residual"
            v.wait_ge(gemm_done, 14 - c.chunk0)
            v.wait_ge(x_loaded, 16)
            v.tensor_tensor(x2n[:R, :], S[:R, :], x[:R, :], ALU.add).then_inc(x2_ready, 1)
            yield "rms2"
            v.wait_ge(sq2_done, 1)
            v.tensor_scalar(ss[:R, :], ss[:R, :], 1.0 / D, EPS, ALU.mult, ALU.add).then_inc(rms2_ready, 1)
            yield "scale2"
            v.wait_ge(rms2_ready, 2)
            do(v.reciprocal(rstd[:R, :], ss[:R, :]))
            v.scalar_tensor_tensor(xtn[:R, :], x2n[:R, :], rstd[:R, 0:1], g_ffn[:R, :], ALU.mult, ALU.mult).then_inc(xt_ready, 1)
            add, settle = chain.add, chain.settle
            for h in range(PH + 1):
                yield f"top{h}"
                best, look = h < PH, h >= 1
                if best:
                    v.wait_ge(ks_ready, h + 1)
                    kq = [ks[:R, h % 2, q * PKEYS:(q + 1) * PKEYS] for q in range(2)]
                    for q in range(2):
                        add(v.max(pick[:R, q, 0:8], kq[q]))
                if look:
                    add(v.tensor_scalar(cij[:R, 0, :], ci[:R, :], 4, None, ALU.logical_shift_right))
                    add(v.tensor_scalar(cij[:R, 1, :], ci[:R, :], TOPK - 1, None, ALU.bitwise_and))
                    add(v.tensor_copy(pickf[:R, :, :], picki[:R, :, :]))
                settle()
                if best:
                    for q in range(2):
                        add(v.max_index(picki[:R, q, 0:8], pick[:R, q, 0:8], kq[q]))
                        ins = v.match_replace(left[:R, q, :], pick[:R, q, 0:8], kq[q], GONE)
                        if q == 0:
                            add(ins)
                        else:
                            ins.then_inc(picked, 1)
                if look:
                    add(v.tensor_copy(cijf[:R, :, :], cij[:R, :, :]))
                settle()
                if best:
                    v.wait_ge(picked, h + 1)
                    for q in range(2):
                        add(v.max(pick[:R, q, 8:16], left[:R, q, :]))
                if look:
                    add(v.tensor_tensor(onehot[:R], iota16[:R, :].unsqueeze(1).unsqueeze(1).to_broadcast([R, 2, TOPK, TOPK]),
                                        cijf[:R, :, :].unsqueeze(3).to_broadcast([R, 2, TOPK, TOPK]), ALU.is_equal))
                settle()
                if best:
                    for q in range(2):
                        add(v.max_index(picki[:R, q, 8:16], pick[:R, q, 8:16], left[:R, q, :]))
                    add(v.tensor_tensor(cand[:R, :, :], pick[:R, 0, :].unsqueeze(2).to_broadcast([R, TOPK, TOPK]),
                                        pick[:R, 1, :].unsqueeze(1).to_broadcast([R, TOPK, TOPK]), ALU.add))
                if look:
                    add(v.tensor_tensor(onehot[:R], onehot[:R], pickf[:R, :, :].unsqueeze(2).to_broadcast([R, 2, TOPK, TOPK]), ALU.mult))
                settle()
                cands = cand[:R, :, :].rearrange("p i j -> p (i j)")
                if best:
                    add(v.max(sc[:R, h, 0:8], cands))
                if look:
                    add(v.tensor_reduce(e12[:R, :, :], onehot[:R], AX, ALU.add))
                settle()
                if best:
                    add(v.max_index(ci[:R, 0:8], sc[:R, h, 0:8], cands))
                    add(v.match_replace(candleft[:R, :], sc[:R, h, 0:8], cands, GONE))
                if look:
                    ins = v.scalar_tensor_tensor(idxn[:R, h - 1, :], e12[:R, 0, :], float(PKEYS), e12[:R, 1, :], ALU.mult, ALU.add)
                    if h == 1:
                        ins.then_inc(first_picked, 1)
                        v.wait_ge(first_picked, 1)
                    else:
                        add(ins)
                settle()
                if best:
                    add(v.max(sc[:R, h, 8:16], candleft[:R, :]))
                    settle()
                    add(v.max_index(ci[:R, 8:16], sc[:R, h, 8:16], candleft[:R, :]))
                    settle()
            yield "gate0"
            v.tensor_tensor(ex[:R, :, :], sc[:R, :, :], sc[:R, :, 0:1].to_broadcast([R, PH, TOPK]), ALU.subtract).then_inc(diff_ready, 1)
            yield "gate2"
            v.wait_ge(ex_ready, 1)
            do(v.tensor_reduce(esum[:R, :], ex[:R, :, :], AX, ALU.add))
            do(v.reciprocal(esum[:R, :], esum[:R, :]))
            do(v.tensor_tensor(gaten[:R, :, :], ex[:R, :, :], esum[:R, :].unsqueeze(2).to_broadcast([R, PH, TOPK]), ALU.mult))


        def wait_v_used(eng, e, m):
            if e.on_vector(m):
                eng.wait_ge(v_added, e.vector_slots(m))
            else:
                eng.wait_ge(v_used, e.tensor_slots(m))

        def gather_u(pool, R, n, index):
            pool.indirect_dma_start(urow[:R, n % NU, :], None, d_peer_u[0], bass.IndirectOffsetOnAxis(ap=index, axis=0)).then_inc(u_landed[n % NU], 16)

        def gathers(pool, e, c):
            if e is not None:
                if e.groups == 1:
                    for n in range(AHEAD, NU):
                        gather_u(pool, P, n, idxn[:, 0, n:n + 1])
                    pool.wait_ge(copied, 2)
                    asked = NU
                else:
                    pool.wait_ge(idx_spread, 16 * e.groups)
                    asked = 0
                for n in range(asked, e.steps):
                    if n < e.slots:
                        if n >= NU:
                            pool.wait_ge(dots, n - NU + 1)
                        gather_u(pool, P, n, idx[:, n:n + 1])
                    m = n - VLAG
                    if m >= 0:
                        if m >= NV:
                            wait_v_used(pool, e, m - NV)
                        pool.indirect_dma_start(vrow[:, m % NV, :], None, d_peer_v[0], bass.IndirectOffsetOnAxis(ap=idx[:, m:m + 1], axis=0)).then_inc(v_landed[m % NV], 16)
            ahead = AHEAD if c is not None and not c.sample else 0
            if ahead:
                pool.wait_ge(first_picked, 1)
                if e is not None:
                    pool.wait_ge(dots, e.slots)
                for n in range(ahead):
                    gather_u(pool, P, n, idxn[:, 0, n:n + 1])
            for i in range(NU):
                turns = (e.landings(e.slots - 1 - (e.slots - 1 - i) % NU) if e is not None else 0) + (i < ahead)
                if turns:
                    pool.wait_ge(u_landed[i], 16 * turns)
            if e is not None:
                for i in range(NV):
                    pool.wait_ge(v_landed[i], 16 * ((e.slots - 1 - i) // NV + 1))
            pool.dma_reset()

        def spread_sync(sp, e):
            indices, gates = idxn.rearrange("p h k -> p (h k)"), gaten.rearrange("p h k -> p (h k)")
            gate_flat = gate.rearrange("p h k -> p (h k)")
            for dst, src, signal in ((idx, indices, idx_spread), (xt, None, xt_spread), (gate_flat, gates, gate_spread)):
                for i in range(e.groups):
                    rows = slice(i * e.tokens, (i + 1) * e.tokens)
                    if src is None:
                        sp.dma_start(dst[rows, :], xtn[:e.tokens, :]).then_inc(signal, 16)
                    else:
                        sp.dma_start(dst[rows, 0:e.slots], src[:e.tokens, i * e.slots:(i + 1) * e.slots]).then_inc(signal, 16)

        def experts_vector(v, e):
            if e.groups == 1:
                v.tensor_copy(xt[:, :], xtn[:, :]).then_inc(copied, 1)
                v.tensor_copy(idx[:, :], idxn[:, :, :].rearrange("p h k -> p (h k)")).then_inc(copied, 1)
                v.tensor_copy(gate[:, :, :], gaten[:, :, :]).then_inc(copied, 1)
                v.wait_ge(copied, 3)
            else:
                v.memset(acc2[:, :], 0.0).then_inc(acc2_zeroed, 1)
                v.wait_ge(xt_spread, 16 * e.groups)
                v.wait_ge(gate_spread, 16 * e.groups)
            for n in range(e.steps):
                yield n
                if n < e.slots:
                    if e.landings(n):
                        v.wait_ge(u_landed[n % NU], 16 * e.landings(n))
                    u = urow[:, n % NU, :]
                    v.tensor_tensor_reduce(u, u, xt[:, :], 1.0, 0.0, ALU.mult, ALU.add, act[:, n // TOPK, n % TOPK:n % TOPK + 1]).then_inc(dots, 1)
                if n % TOPK == 4 and TOPK <= n < e.slots + TOPK:
                    h = n // TOPK - 1
                    v.wait_ge(gelu_done, h + 1)
                    v.tensor_tensor(wgt[:, h * TOPK:(h + 1) * TOPK], gel[:, h, :], gate[:, h, :], ALU.mult).then_inc(wgt_ready, 1)
                m = n - VLAG
                if m >= 0 and e.on_vector(m):
                    v.wait_ge(v_landed[m % NV], 16 * (m // NV + 1))
                    v.wait_ge(wgt_ready, m // TOPK + 1)
                    if e.vector_slots(m) == 1:
                        v.wait_ge(x2_copied, 1)
                    else:
                        v.wait_ge(v_added, e.vector_slots(m) - 1)
                    v.scalar_tensor_tensor(acc2[:, :], vrow[:, m % NV, :], wgt[:, m:m + 1], acc2[:, :], ALU.mult, ALU.add).then_inc(v_added, 1)
            last = e.slots - 1
            if e.groups == 1:
                v.wait_ge(v_added, e.vector_slots(last))
                v.wait_ge(v_used, e.tensor_slots(last))
                v.tensor_tensor(acc2[:, :], acc2[:, :], acc[:, :], ALU.add).then_inc(y_ready, 1)
            else:
                v.wait_ge(v_used, e.tensor_slots(last) + 1)
                v.tensor_copy(acc2[:e.tokens, :], acc[:e.tokens, :]).then_inc(y_ready, 1)

        def experts_scalar(sc_, e):
            if e.groups > 1:
                sc_.wait_ge(acc2_zeroed, 1)
            sc_.activation(acc2[:e.tokens, :], x2n[:e.tokens, :], ACT.Copy).then_inc(x2_copied, 1)
            places = ident if e.groups == 1 else fold
            for n in range(e.steps):
                yield n
                if n % TOPK == 2 and TOPK <= n < e.slots + TOPK:
                    h = n // TOPK - 1
                    sc_.wait_ge(dots, (h + 1) * TOPK)
                    sc_.activation(gel[:, h, :], act[:, h, :], ACT.Gelu).then_inc(gelu_done, 1)
                m = n - VLAG + 2
                if 0 <= m < e.slots and not e.on_vector(m):
                    j = e.tensor_slots(m) - 1
                    sc_.wait_ge(wgt_ready, m // TOPK + 1)
                    if j >= ND:
                        sc_.wait_ge(v_used, j - ND + 1)
                    sc_.activation(diag[:, j % ND, :e.tokens], places[:, :e.tokens], ACT.Copy, scale=wgt[:, m:m + 1]).then_inc(diag_ready, 1)

        def experts_tensor(pe, e):
            last = e.tensor_slots(e.slots - 1) - 1
            for n in range(e.steps):
                yield n
                m = n - VLAG
                if m >= 0 and not e.on_vector(m):
                    j = e.tensor_slots(m) - 1
                    pe.wait_ge(diag_ready, j + 1)
                    pe.wait_ge(v_landed[m % NV], 16 * (m // NV + 1))
                    for i in range(2):
                        ins = pe.matmul(acc[:e.tokens, i * BANK:(i + 1) * BANK], diag[:, j % ND, :e.tokens], vrow[:, m % NV, i * BANK:(i + 1) * BANK],
                                        start=j == 0, stop=j == last and e.groups == 1)
                    ins.then_inc(v_used, 1)
            if e.groups > 1:
                pe.wait_ge(v_added, e.vector_slots(e.slots - 1))
                for i in range(2):
                    ins = pe.matmul(acc[:e.tokens, i * BANK:(i + 1) * BANK], fold[:, :], acc2[:, i * BANK:(i + 1) * BANK], start=False, stop=True)
                ins.then_inc(v_used, 1)

        def block_of(e, c):
            def both(experts, prepare):
                beside(experts if experts is not None else [], [prepare, None] if prepare is not None else None, AT[c.kind] if c is not None else None)

            with nc.Block() as block:
                @block.sync
                def _(sp):
                    if e is not None and e.groups > 1:
                        spread_sync(sp, e)
                    if c is not None:
                        prepare_sync(sp, e, c)
                    if e is not None:
                        sp.wait_ge(y_ready, 1)
                        sp.dma_start(e.y_out, acc2[:e.tokens, :]).then_inc(y_stored, 16)
                        sp.wait_ge(y_stored, 16)

                @block.gpsimd
                def _(pool):
                    gathers(pool, e, c)

                @block.vector
                def _(v):
                    both(experts_vector(v, e) if e is not None else None, prepare_vector(v, c, Chain(v, dve_chain)) if c is not None else None)

                @block.scalar
                def _(sc_):
                    both(experts_scalar(sc_, e) if e is not None else None, prepare_scalar(sc_, c) if c is not None else None)

                @block.tensor
                def _(pe):
                    both(experts_tensor(pe, e) if e is not None else None, prepare_tensor(pe, c) if c is not None else None)
            end_block()

        def prompt_tile(t, blocks, kind, mate=None):
            rows = bass.ds(t * P, P)
            return NextTile(
                kind, mate, rows=P, blocks=blocks, sample=False, x_in=d_x_prompt[0][rows, :],
                own_keys=lambda m: m[:, rows], own_keysT=kT[:, :, rows], own_negF=negF[0:AH, rows],
                own_values=v_all[:, bass.ds(t, 1), :].rearrange("p a n -> p (a n)"),
                k_out=d_a_k[0][0][rows].rearrange("n h d -> n (h d)"), v_out=d_a_v[0][0][rows].rearrange("n h d -> n (h d)"),
                logf_out=d_a_logf[0][0][rows, :], conv_out=d_b_conv[0][0])

        sample_tile = NextTile(
            SECOND, None, rows=NEW, blocks=3, sample=True, x_in=d_x_sample[0],
            own_keys=lambda m: m[:, PAST:PAST + NEW], own_keysT=kT[:, :, PAST:PAST + NEW], own_negF=negF[0:AH, PAST:PAST + NEW],
            own_values=v_all[0:NEW, 2, :],
            k_out=d_a_k_s[0][0].rearrange("n h d -> n (h d)"), v_out=d_a_v_s[0][0].rearrange("n h d -> n (h d)"),
            logf_out=d_a_logf_s[0][0], conv_out=d_b_conv_s[0][0])

        def prompt_experts(t, beside):
            return Tile(P, d_y_prompt[0][bass.ds(t * P, P), :], beside)

        def pair(t, blocks):
            block_of(prompt_experts(t - 1, FIRST), prompt_tile(t, blocks, FIRST, Mate(P, d_x_prompt[0][bass.ds((t + 1) * P, P), :])))
            block_of(prompt_experts(t, SECOND), prompt_tile(t + 1, blocks, SECOND))

        setup()
        block_of(None, prompt_tile(0, 1, ALONE))
        with nc.Fori(0, 2) as i:
            pair(2 * i + 1, 5)
        pair(5, 7)
        block_of(prompt_experts(6, FIRST), prompt_tile(7, TILES, FIRST, Mate(NEW, d_x_sample[0])))
        block_of(prompt_experts(7, SECOND), sample_tile)
        block_of(Tile(NEW, d_y_sample[0]), None)


_INS = ['x_prompt', 'x_sample', 'cache_a_k', 'cache_a_v', 'cache_a_logf', 'cache_b_conv', 'cache_m_k', 'cache_m_v',
        'mem_prompt', 'g_attn', 'w_in', 'b_f', 'g_q_a', 'g_k_a', 'conv_w', 'conv_b', 'g_mem', 'w_mem_k', 'w_mem_v',
        'g_k_m', 'g_q_m', 'w_out', 'g_ffn', 'w_peer_q', 'peer_keys', 'peer_u', 'peer_v']
_OUTS = [('y_prompt', (1, 1024, 1024)), ('y_sample', (1, 32, 1024)), ('a_k', (1, 1, 1024, 8, 64)), ('a_v', (1, 1, 1024, 8, 64)),
         ('a_logf', (1, 1, 1024, 8)), ('b_conv', (1, 1, 2, 256)), ('m_k', (1, 1, 256, 4, 64)), ('m_v', (1, 1, 256, 4, 64)),
         ('a_k_s', (1, 1, 32, 8, 64)), ('a_v_s', (1, 1, 32, 8, 64)), ('a_logf_s', (1, 1, 32, 8)), ('b_conv_s', (1, 1, 2, 256))]


def kernel(**inputs):
    import numpy as _np
    import concourse.bacc as _bacc
    from concourse import mybir as _mybir
    from concourse.bass_utils import run_bass_kernel_spmd as _run

    nc = _bacc.Bacc("TRN2", target_bir_lowering=False, num_devices=1)
    arrays, args = {}, []
    for name in _INS:
        v = _np.ascontiguousarray(inputs[name])
        arrays[f"in_{name}_dram"] = v
        args.append(nc.dram_tensor(f"in_{name}_dram", v.shape, _mybir.dt.from_np(v.dtype), kind="ExternalInput").ap())
    for name, shape in _OUTS:
        args.append(nc.dram_tensor(f"out_{name}_dram", shape, F32, kind="ExternalOutput").ap())
    build(nc, *args)
    r = _run(nc, [arrays], core_ids=[0])
    return tuple(r.results[0][f"out_{name}_dram"] for name, _ in _OUTS)
```
